# Optimizing a Trainium2 kernel written in Bass

```python
import math
import jax, jax.numpy as jnp
from jax import lax
import numpy as np
import jax
import jax.numpy as jnp

D_MODEL = 1024
BATCH = 1
SEQ = 512
DEPTH = 2

CTX_LEN = 256
GRID_W = 64
EPS = 1e-6
NEG_INF = -1e30

GLA_HEADS = 6
GLA_DK = 32
GLA_DV = 64
GLA_LOWRANK = 16
GLA_TAU = 16.0
GLA_CHUNK = 16
ROPE_BASE = 10000.0
SC_WIDTH = 256
SC_GROUPS = 4
NA_HEADS = 6
NA_DH = 64
NA_WIN_ROWS = 8
NA_WIN_COLS = 16
FFN_DIM = 2816

GLA_QK = GLA_HEADS * GLA_DK
GLA_V = GLA_HEADS * GLA_DV
NA_W = NA_HEADS * NA_DH
MIX_WIDTH = GLA_V + SC_WIDTH + NA_W
IN_SPLIT = (GLA_QK, GLA_QK, GLA_V, GLA_LOWRANK, GLA_LOWRANK, GLA_V,
            SC_WIDTH, SC_WIDTH, SC_WIDTH, NA_W, NA_W, NA_W)
IN_WIDTH = 2 * GLA_QK + 2 * GLA_V + 2 * GLA_LOWRANK + 3 * SC_WIDTH + 3 * NA_W


def rmsnorm(t, g):
    tf = t.astype(jnp.float32)
    y = tf * lax.rsqrt(jnp.mean(tf * tf, axis=-1, keepdims=True) + EPS)
    return (y * g.astype(jnp.float32)).astype(t.dtype)

def modulate(t, shift, scale):
    return t * (1 + scale) + shift

def split_cols(u):
    parts, start = [], 0
    for size in IN_SPLIT:
        parts.append(u[..., start:start + size])
        start += size
    return parts

def dwconv3(t, w, b):
    tp = jnp.pad(t, ((0, 0), (1, 1), (0, 0)))
    return tp[:, :-2] * w[0] + tp[:, 1:-1] * w[1] + tp[:, 2:] * w[2] + b

def axial_rope(n_tokens, dim):
    t = jnp.arange(n_tokens)
    n_freq = dim // 4
    inv_freq = ROPE_BASE ** (-jnp.arange(n_freq, dtype=jnp.float32) / n_freq)
    row = (t // GRID_W).astype(jnp.float32)[:, None] * inv_freq
    col = (t % GRID_W).astype(jnp.float32)[:, None] * inv_freq
    ang = jnp.concatenate([row, col], axis=-1)
    return jnp.cos(ang)[None, :, None, :], jnp.sin(ang)[None, :, None, :]

def apply_rope(t, cos, sin):
    t1, t2 = t[..., 0::2], t[..., 1::2]
    return jnp.stack([t1 * cos - t2 * sin, t1 * sin + t2 * cos], axis=-1).reshape(t.shape)

def gla_chunked(q, k, v, g, s0):
    bsz, n_tok, h, dk = q.shape
    dv = v.shape[-1]
    n_chunks = n_tok // GLA_CHUNK
    rs = lambda t: t.reshape(bsz, n_chunks, GLA_CHUNK, h, t.shape[-1])
    q, k, v, g = rs(q), rs(k), rs(v), rs(g)
    b = jnp.cumsum(g, axis=2)
    b_last = b[:, :, -1:]
    q_dec = q * jnp.exp(b)
    k_inv = k * jnp.exp(-b)
    k_end = k * jnp.exp(b_last - b)
    causal = jnp.tril(jnp.ones((GLA_CHUNK, GLA_CHUNK), dtype=bool))
    a = jnp.einsum('bnihk,bnjhk->bnhij', q_dec, k_inv)
    a = jnp.where(causal, a, 0.0)
    o_intra = jnp.einsum('bnhij,bnjhv->bnihv', a, v)

    def step(s, xs):
        qd, ke, vv, dec = xs
        o = jnp.einsum('bihk,bhkv->bihv', qd, s)
        s = s * dec[..., None] + jnp.einsum('bjhk,bjhv->bhkv', ke, vv)
        return s, o

    xs = (jnp.moveaxis(q_dec, 1, 0), jnp.moveaxis(k_end, 1, 0), jnp.moveaxis(v, 1, 0),
          jnp.moveaxis(jnp.exp(b_last[:, :, 0]), 1, 0))
    s_final, o_inter = lax.scan(step, s0, xs)
    o = o_intra + jnp.moveaxis(o_inter, 0, 1)
    return o.reshape(bsz, n_tok, h, dv), s_final

def gla_prep(q, k, v, glr_f, glr_b, wg2_fw, bg_fw, wg2_bw, bg_bw, rope):
    bsz, n_tok, _ = q.shape
    heads = lambda t, d: t.astype(jnp.float32).reshape(bsz, n_tok, GLA_HEADS, d)
    q = heads(q, GLA_DK) * (GLA_DK ** -0.5)
    k = heads(k, GLA_DK)
    v = heads(v, GLA_DV)
    if rope is not None:
        q = apply_rope(q, rope[0], rope[1])
        k = apply_rope(k, rope[0], rope[1])
    g_f = heads(jax.nn.log_sigmoid((glr_f @ wg2_fw + bg_fw).astype(jnp.float32)), GLA_DK) / GLA_TAU
    g_b = heads(jax.nn.log_sigmoid((glr_b @ wg2_bw + bg_bw).astype(jnp.float32)), GLA_DK) / GLA_TAU
    return q, k, v, g_f, g_b

def gla_output(o, r, norm_g):
    of = o * lax.rsqrt(jnp.mean(o * o, axis=-1, keepdims=True) + EPS) * norm_g.astype(jnp.float32)
    bsz, n_tok = o.shape[:2]
    return (of.reshape(bsz, n_tok, GLA_V) * jax.nn.silu(r.astype(jnp.float32))).astype(r.dtype)

def gla_mixer(lat, cpar, rope, wg2_fw, bg_fw, wg2_bw, bg_bw, norm_g, need_ctx_out):
    flip = lambda t: jnp.flip(t, axis=1)
    qc, kc, vc, gfc, gbc = gla_prep(*cpar[:5], wg2_fw, bg_fw, wg2_bw, bg_bw, None)
    ql, kl, vl, gfl, gbl = gla_prep(*lat[:5], wg2_fw, bg_fw, wg2_bw, bg_bw, rope)
    s0 = jnp.zeros((qc.shape[0], GLA_HEADS, GLA_DK, GLA_DV), jnp.float32)
    oc_f, sc_f = gla_chunked(qc, kc, vc, gfc, s0)
    oc_b, sc_b = gla_chunked(flip(qc), flip(kc), flip(vc), flip(gbc), s0)
    ol_f, _ = gla_chunked(ql, kl, vl, gfl, sc_f)
    ol_b, _ = gla_chunked(flip(ql), flip(kl), flip(vl), flip(gbl), sc_b)
    out_lat = gla_output(ol_f + flip(ol_b), lat[5], norm_g)
    out_ctx = gla_output(oc_f + flip(oc_b), cpar[5], norm_g) if need_ctx_out else None
    return out_lat, out_ctx

def short_conv(b_gate, c_gate, xh, w, bias):
    return b_gate * dwconv3(c_gate * xh, w, bias)

def neighbourhood_attention(q, k, v, k_ctx, v_ctx, rpb):
    bsz, n_tok, _ = q.shape
    rows = n_tok // GRID_W
    kh = min(NA_WIN_ROWS, rows)
    kw = NA_WIN_COLS
    grid = lambda t: t.reshape(bsz, rows, GRID_W, NA_HEADS, NA_DH)
    qg = grid(q.astype(jnp.float32) * (NA_DH ** -0.5))
    kg, vg = grid(k), grid(v)
    kc = k_ctx.reshape(bsz, -1, NA_HEADS, NA_DH).astype(jnp.float32)
    vc = v_ctx.reshape(bsz, -1, NA_HEADS, NA_DH).astype(jnp.float32)
    col = jnp.arange(GRID_W)
    col_start = jnp.clip(col - kw // 2, 0, GRID_W - kw)
    col_mask = (col[None, :] >= col_start[:, None]) & (col[None, :] < col_start[:, None] + kw)
    dc_idx = jnp.clip(col[None, :] - col[:, None] + NA_WIN_COLS - 1, 0, 2 * NA_WIN_COLS - 2)
    rpb_cols = jnp.take(rpb.astype(jnp.float32), dc_idx, axis=2)

    def row_block(r):
        rs = jnp.clip(r - kh // 2, 0, rows - kh)
        q_r = lax.dynamic_index_in_dim(qg, r, axis=1, keepdims=False)
        k_band = lax.dynamic_slice_in_dim(kg, rs, kh, axis=1).astype(jnp.float32)
        v_band = lax.dynamic_slice_in_dim(vg, rs, kh, axis=1).astype(jnp.float32)
        dr_idx = rs + jnp.arange(kh) - r + NA_WIN_ROWS - 1
        bias = jnp.take(rpb_cols, dr_idx, axis=1)
        s_loc = jnp.einsum('bqhd,bikhd->bhqik', q_r, k_band) + jnp.transpose(bias, (0, 2, 1, 3))[None]
        s_loc = jnp.where(col_mask[None, None, :, None, :], s_loc, NEG_INF)
        s_ctx = jnp.einsum('bqhd,bchd->bhqc', q_r, kc)
        s = jnp.concatenate([s_loc.reshape(bsz, NA_HEADS, GRID_W, kh * GRID_W), s_ctx], axis=-1)
        p = jax.nn.softmax(s, axis=-1)
        p_loc = p[..., :kh * GRID_W].reshape(bsz, NA_HEADS, GRID_W, kh, GRID_W)
        p_ctx = p[..., kh * GRID_W:]
        o = jnp.einsum('bhqik,bikhd->bqhd', p_loc, v_band) + jnp.einsum('bhqc,bchd->bqhd', p_ctx, vc)
        return o.astype(q.dtype)

    out = lax.map(row_block, jnp.arange(rows))
    return jnp.moveaxis(out, 0, 1).reshape(bsz, n_tok, NA_W)

def context_attention(q, k, v):
    bsz, n_tok, _ = q.shape
    hs = lambda t: t.astype(jnp.float32).reshape(bsz, n_tok, NA_HEADS, NA_DH)
    s = jnp.einsum('bqhd,bkhd->bhqk', hs(q) * (NA_DH ** -0.5), hs(k))
    o = jnp.einsum('bhqk,bkhd->bqhd', jax.nn.softmax(s, axis=-1), hs(v))
    return o.reshape(bsz, n_tok, NA_W).astype(q.dtype)

def conv_ffn(h, w_up, cw, cb, w_down):
    u = dwconv3(h @ w_up, cw, cb)
    a, b = jnp.split(u, 2, axis=-1)
    return (jax.nn.silu(a) * b) @ w_down

def first_inputs(seed: int = 0) -> dict:
    key = jax.random.key(seed)
    ks = jax.random.split(key, 24)
    nrm = lambda k, shape, s: jax.random.normal(k, shape, jnp.float32) * s
    return {
        "x": nrm(ks[0], (BATCH, SEQ, D_MODEL), 1.0),
        "c": nrm(ks[1], (BATCH, D_MODEL), 1.0),
        "ctx": nrm(ks[2], (BATCH, CTX_LEN, D_MODEL), 1.0),
        "c_ctx": nrm(ks[3], (D_MODEL,), 1.0),
        "w_ada": nrm(ks[4], (DEPTH, D_MODEL, 6 * D_MODEL), 0.5 * D_MODEL ** -0.5),
        "b_ada": nrm(ks[5], (DEPTH, 6 * D_MODEL), 0.02),
        "norm_mix_g": 1.0 + nrm(ks[6], (DEPTH, D_MODEL), 0.05),
        "norm_ffn_g": 1.0 + nrm(ks[7], (DEPTH, D_MODEL), 0.05),
        "w_in": nrm(ks[8], (DEPTH, D_MODEL, IN_WIDTH), D_MODEL ** -0.5),
        "gla_wg2_fw": nrm(ks[9], (DEPTH, GLA_LOWRANK, GLA_QK), GLA_LOWRANK ** -0.5),
        "gla_bg_fw": nrm(ks[10], (DEPTH, GLA_QK), 0.02),
        "gla_wg2_bw": nrm(ks[11], (DEPTH, GLA_LOWRANK, GLA_QK), GLA_LOWRANK ** -0.5),
        "gla_bg_bw": nrm(ks[12], (DEPTH, GLA_QK), 0.02),
        "gla_norm_g": 1.0 + nrm(ks[13], (DEPTH, GLA_DV), 0.05),
        "sc_conv_w": nrm(ks[14], (DEPTH, 3, SC_WIDTH), 3 ** -0.5),
        "sc_conv_b": nrm(ks[15], (DEPTH, SC_WIDTH), 0.02),
        "na_rpb": nrm(ks[16], (DEPTH, NA_HEADS, 2 * NA_WIN_ROWS - 1, 2 * NA_WIN_COLS - 1), 0.02),
        "w_out": nrm(ks[17], (DEPTH, MIX_WIDTH, D_MODEL), MIX_WIDTH ** -0.5),
        "ffn_w_up": nrm(ks[18], (DEPTH, D_MODEL, 2 * FFN_DIM), D_MODEL ** -0.5),
        "ffn_conv_w": nrm(ks[19], (DEPTH, 3, 2 * FFN_DIM), 3 ** -0.5),
        "ffn_conv_b": nrm(ks[20], (DEPTH, 2 * FFN_DIM), 0.02),
        "ffn_w_down": nrm(ks[21], (DEPTH, FFN_DIM, D_MODEL), FFN_DIM ** -0.5),
        "final_norm_g": 1.0 + nrm(ks[22], (D_MODEL,), 0.05),
    }

def first_block(x, c, ctx, c_ctx, w_ada, b_ada, norm_mix_g, norm_ffn_g, w_in, gla_wg2_fw, gla_bg_fw,
              gla_wg2_bw, gla_bg_bw, gla_norm_g, sc_conv_w, sc_conv_b, na_rpb, w_out, ffn_w_up,
              ffn_conv_w, ffn_conv_b, ffn_w_down, final_norm_g):
    n_lat = x.shape[1]
    rope = axial_rope(n_lat, GLA_DK)
    xc = ctx
    for layer in range(DEPTH):
        update_ctx = layer < DEPTH - 1
        mod = jax.nn.silu(c) @ w_ada[layer] + b_ada[layer]
        sh1, sc1, g1, sh2, sc2, g2 = jnp.split(mod[:, None, :], 6, axis=-1)
        modc = jax.nn.silu(c_ctx) @ w_ada[layer] + b_ada[layer]
        sh1c, sc1c, g1c, sh2c, sc2c, g2c = jnp.split(modc, 6, axis=-1)

        u = modulate(rmsnorm(x, norm_mix_g[layer]), sh1, sc1) @ w_in[layer]
        uc = modulate(rmsnorm(xc, norm_mix_g[layer]), sh1c, sc1c) @ w_in[layer]
        lat = split_cols(u)
        cpar = split_cols(uc)
        gla_lat, gla_ctx = gla_mixer(lat[:6], cpar[:6], rope, gla_wg2_fw[layer], gla_bg_fw[layer],
                                     gla_wg2_bw[layer], gla_bg_bw[layer], gla_norm_g[layer], update_ctx)
        sc_lat = short_conv(lat[6], lat[7], lat[8], sc_conv_w[layer], sc_conv_b[layer])
        na_lat = neighbourhood_attention(lat[9], lat[10], lat[11], cpar[10], cpar[11], na_rpb[layer])
        x = x + g1 * (jnp.concatenate([gla_lat, sc_lat, na_lat], axis=-1) @ w_out[layer])
        h = modulate(rmsnorm(x, norm_ffn_g[layer]), sh2, sc2)
        x = x + g2 * conv_ffn(h, ffn_w_up[layer], ffn_conv_w[layer], ffn_conv_b[layer], ffn_w_down[layer])

        if update_ctx:
            sc_ctx = short_conv(cpar[6], cpar[7], cpar[8], sc_conv_w[layer], sc_conv_b[layer])
            na_ctx = context_attention(cpar[9], cpar[10], cpar[11])
            xc = xc + g1c * (jnp.concatenate([gla_ctx, sc_ctx, na_ctx], axis=-1) @ w_out[layer])
            hc = modulate(rmsnorm(xc, norm_ffn_g[layer]), sh2c, sc2c)
            xc = xc + g2c * conv_ffn(hc, ffn_w_up[layer], ffn_conv_w[layer], ffn_conv_b[layer],
                                     ffn_w_down[layer])
    return rmsnorm(x, final_norm_g)


DEPTH_2 = 1

HEAD_DIM = 64
Q_BLOCK = 128

A_HEADS = 4
A_PATTERNS = ((128, 1), (512, 4), (2048, 16))
A_GROUPS = 3
A_WIDTH = A_HEADS * HEAD_DIM

B_HEADS = 4
B_WIDTH = B_HEADS * HEAD_DIM
IDX_HEADS = 4
IDX_DIM = 64
TOPK_MAX = 256

C_HEADS = 4
C_WIDTH = C_HEADS * HEAD_DIM
C_LORA_W = 32
C_LORA_A = 32
C_LORA_G = 64
C_LORA_V = 16
C_IN = 3 * C_WIDTH + C_LORA_W + C_LORA_A + C_LORA_G
C_GN_EPS = 64e-5

D_HEADS = 4
D_INNER = D_HEADS * HEAD_DIM
D_GROUPS = 2
D_STATE = 64
D_CONV = 4
D_CHUNK = 128
D_XBC = D_INNER + 2 * D_GROUPS * D_STATE
D_NORM_EPS = 1e-5

N_BRANCH = 4
BRANCH_WIDTH = 256

N_EXPERT_GROUPS = 4
EXPERTS_PER_GROUP = 8
N_EXPERTS = N_EXPERT_GROUPS * EXPERTS_PER_GROUP
TOP_K_EXPERTS = 2
D_EXPERT = 512
MOE_BLOCK = 128

LN_EPS = 1e-5
DEEPNORM_ALPHA = (2 * DEPTH_2) ** 0.25
DEEPNORM_BETA = (8 * DEPTH_2) ** -0.25

IN_SEGMENTS = (
    ('a_qkv', 3 * A_GROUPS * A_WIDTH),
    ('b_qkv', 3 * B_WIDTH),
    ('b_idx_q', IDX_HEADS * IDX_DIM),
    ('b_idx_k', IDX_DIM),
    ('b_idx_w', IDX_HEADS),
    ('c_in', C_IN),
    ('d_z', D_INNER),
    ('d_xbc', D_XBC),
    ('d_dt', D_HEADS),
    ('gates', N_BRANCH * D_MODEL),
)
IN_WIDTH_2 = sum(size for _, size in IN_SEGMENTS)


def _split(x, sizes):
    out, off = [], 0
    for s in sizes:
        out.append(x[..., off:off + s])
        off += s
    return out

def layer_norm(x, g, b):
    xf = x.astype(jnp.float32)
    mu = jnp.mean(xf, axis=-1, keepdims=True)
    var = jnp.mean(jnp.square(xf - mu), axis=-1, keepdims=True)
    return ((xf - mu) * lax.rsqrt(var + LN_EPS) * g + b).astype(x.dtype)

def dilated_window_attention(qs, ks, vs):
    b, T = qs[0].shape[:2]
    scale = HEAD_DIM ** -0.5
    kps = [jnp.pad(k, ((0, 0), (w, 0), (0, 0), (0, 0))) for k, (w, _) in zip(ks, A_PATTERNS)]
    vps = [jnp.pad(v, ((0, 0), (w, 0), (0, 0), (0, 0))) for v, (w, _) in zip(vs, A_PATTERNS)]

    def block(i):
        start = i * Q_BLOCK
        outs, lses = [], []
        for q, kp, vp, (win, dil) in zip(qs, kps, vps, A_PATTERNS):
            nq, nk, span = Q_BLOCK // dil, win // dil, (win + Q_BLOCK) // dil
            qb = lax.dynamic_slice_in_dim(q, start, Q_BLOCK, axis=1).reshape(b, nq, dil, A_HEADS, HEAD_DIM)
            kb = lax.dynamic_slice_in_dim(kp, start, win + Q_BLOCK, axis=1).reshape(b, span, dil, A_HEADS, HEAD_DIM)
            vb = lax.dynamic_slice_in_dim(vp, start, win + Q_BLOCK, axis=1).reshape(b, span, dil, A_HEADS, HEAD_DIM)
            s = jnp.einsum('barhe,bcrhe->brhac', qb, kb).astype(jnp.float32) * scale
            a_idx = jnp.arange(nq)[:, None]
            c_idx = jnp.arange(span)[None, :]
            band = (c_idx >= a_idx) & (c_idx <= a_idx + nk)
            key_pos = start - win + jnp.arange(span)[None, :] * dil + jnp.arange(dil)[:, None]
            ok = band[None, :, :] & (key_pos >= 0)[:, None, :]
            s = jnp.where(ok[None, :, None], s, -jnp.inf)
            lse = jax.nn.logsumexp(s, axis=-1)
            p = jnp.exp(s - lse[..., None]).astype(vb.dtype)
            o = jnp.einsum('brhac,bcrhe->barhe', p, vb).reshape(b, Q_BLOCK, A_HEADS, HEAD_DIM)
            outs.append(o)
            lses.append(lse.transpose(0, 3, 1, 2).reshape(b, Q_BLOCK, A_HEADS))
        mix = jax.nn.softmax(jnp.stack(lses), axis=0)
        out = mix[0][..., None].astype(outs[0].dtype) * outs[0]
        for g in range(1, A_GROUPS):
            out = out + mix[g][..., None].astype(outs[g].dtype) * outs[g]
        return out

    out = lax.map(block, jnp.arange(T // Q_BLOCK))
    return out.transpose(1, 0, 2, 3, 4).reshape(b, T, A_WIDTH)

def indexer_sparse_attention(q, k, v, iq, ik, iw):
    b, T = q.shape[:2]
    top_k = min(TOPK_MAX, T // 4)
    scale = HEAD_DIM ** -0.5
    key_pos = jnp.arange(T)
    gather = jax.vmap(lambda arr, idx: arr[idx])

    def block(i):
        start = i * Q_BLOCK
        t = start + jnp.arange(Q_BLOCK)
        qi = lax.dynamic_slice_in_dim(iq, start, Q_BLOCK, axis=1)
        wi = lax.dynamic_slice_in_dim(iw, start, Q_BLOCK, axis=1).astype(jnp.float32)
        logits = jnp.einsum('bqhd,bsd->bqhs', qi, ik).astype(jnp.float32) * IDX_DIM ** -0.5
        score = jnp.einsum('bqhs,bqh->bqs', jax.nn.relu(logits), wi) * IDX_HEADS ** -0.5
        score = jnp.where((key_pos[None, :] <= t[:, None])[None], score, -jnp.inf)
        _, sel = lax.top_k(score, top_k)
        valid = sel <= t[None, :, None]
        kg = gather(k, sel)
        vg = gather(v, sel)
        qb = lax.dynamic_slice_in_dim(q, start, Q_BLOCK, axis=1)
        s = jnp.einsum('bqhe,bqjhe->bhqj', qb, kg).astype(jnp.float32) * scale
        s = jnp.where(valid[:, None], s, -jnp.inf)
        p = jax.nn.softmax(s, axis=-1).astype(vg.dtype)
        return jnp.einsum('bhqj,bqjhe->bqhe', p, vg)

    out = lax.map(block, jnp.arange(T // Q_BLOCK))
    return out.transpose(1, 0, 2, 3, 4).reshape(b, T, B_WIDTH)

def token_shift(x):
    return jnp.pad(x, ((0, 0), (1, 0), (0, 0)))[:, :-1]

def wkv7_scan(r, w, k, v, a, bb):
    b, T, H, N = r.shape

    def step(state, inp):
        rt, wt, kt, vt, at, bt = inp
        sa = jnp.einsum('bhij,bhj->bhi', state, at)
        state = state * wt[:, :, None, :] + sa[..., None] * bt[:, :, None, :] + vt[..., None] * kt[:, :, None, :]
        return state, jnp.einsum('bhij,bhj->bhi', state, rt)

    seq_major = tuple(jnp.moveaxis(t.astype(jnp.float32), 1, 0) for t in (r, w, k, v, a, bb))
    _, y = lax.scan(step, jnp.zeros((b, H, N, N), jnp.float32), seq_major)
    return jnp.moveaxis(y, 0, 1)

def rwkv7_time_mix(pc, mu, w0, w2, a0, a2, g2, k_k, k_a, r_k, gn_w, gn_b, v_first, v_lora):
    b, T, _ = pc.shape
    pc = pc + (token_shift(pc) - pc) * mu
    r, k, v, xw, xa, xg = _split(pc, (C_WIDTH, C_WIDTH, C_WIDTH, C_LORA_W, C_LORA_A, C_LORA_G))
    w = -jax.nn.softplus(-(w0 + jnp.tanh(xw) @ w2)) - 0.5
    a = jax.nn.sigmoid(a0 + xa @ a2)
    g = jax.nn.sigmoid(xg) @ g2
    if v_lora is not None:
        v0, v1, v2 = v_lora
        v = v + (v_first - v) * jax.nn.sigmoid(v0 + (v @ v1) @ v2)
    heads = lambda t: t.astype(jnp.float32).reshape(b, T, C_HEADS, HEAD_DIM)
    kk = heads(k * k_k)
    kk = kk / jnp.maximum(jnp.linalg.norm(kk, axis=-1, keepdims=True), 1e-12)
    k_mod = heads(k * (1.0 + (a - 1.0) * k_a))
    r_h, v_h, a_h = heads(r), heads(v), heads(a)
    decay = jnp.exp(-jnp.exp(heads(w)))
    y = wkv7_scan(r_h, decay, k_mod, v_h, -kk, kk * a_h)
    y_mu = jnp.mean(y, axis=-1, keepdims=True)
    y_var = jnp.mean(jnp.square(y - y_mu), axis=-1, keepdims=True)
    y = ((y - y_mu) * lax.rsqrt(y_var + C_GN_EPS)).reshape(b, T, C_WIDTH) * gn_w + gn_b
    bonus = jnp.sum(r_h * k_mod * r_k, axis=-1, keepdims=True) * v_h
    o = (y + bonus.reshape(b, T, C_WIDTH)) * g
    return o.astype(pc.dtype), v

def ssd_chunked(x, a, bm, cm):
    b, T, H, P = x.shape
    nc = T // D_CHUNK
    x = x.reshape(b, nc, D_CHUNK, H, P)
    bm = bm.reshape(b, nc, D_CHUNK, H, -1)
    cm = cm.reshape(b, nc, D_CHUNK, H, -1)
    a_cs = jnp.cumsum(a.reshape(b, nc, D_CHUNK, H).transpose(0, 3, 1, 2), axis=-1)
    seg = a_cs[..., :, None] - a_cs[..., None, :]
    causal = jnp.tril(jnp.ones((D_CHUNK, D_CHUNK), dtype=bool))
    decay_ls = jnp.exp(jnp.where(causal, seg, -jnp.inf))
    scores = jnp.einsum('bclhn,bcshn->bhcls', cm, bm) * decay_ls
    y_diag = jnp.einsum('bhcls,bcshp->bclhp', scores, x)
    decay_to_end = jnp.exp(a_cs[..., -1:] - a_cs)
    chunk_states = jnp.einsum('bclhn,bhcl,bclhp->bchpn', bm, decay_to_end, x)
    chunk_decay = jnp.exp(a_cs[..., -1])

    def step(state, inp):
        st, dc = inp
        return state * dc[..., None, None] + st, state

    _, states_in = lax.scan(step, jnp.zeros((b, H, P, bm.shape[-1]), jnp.float32),
                            (jnp.moveaxis(chunk_states, 1, 0), jnp.moveaxis(chunk_decay, 2, 0)))
    states_in = jnp.moveaxis(states_in, 0, 1)
    y_off = jnp.einsum('bclhn,bchpn,bhcl->bclhp', cm, states_in, jnp.exp(a_cs))
    return (y_diag + y_off).reshape(b, T, H, P)

def mamba2_mixer(z, xbc, dt_raw, conv_w, conv_b, dt_bias, a_log, d_skip, norm_w):
    b, T, _ = z.shape
    xbc = lax.conv_general_dilated(xbc, conv_w[:, None, :], window_strides=(1,),
                                   padding=[(D_CONV - 1, 0)],
                                   dimension_numbers=('NWC', 'WIO', 'NWC'),
                                   feature_group_count=D_XBC)
    xbc = jax.nn.silu(xbc + conv_b).astype(jnp.float32)
    heads_per_group = D_HEADS // D_GROUPS
    xs = xbc[..., :D_INNER].reshape(b, T, D_HEADS, HEAD_DIM)
    bm = xbc[..., D_INNER:D_INNER + D_GROUPS * D_STATE].reshape(b, T, D_GROUPS, D_STATE)
    cm = xbc[..., D_INNER + D_GROUPS * D_STATE:].reshape(b, T, D_GROUPS, D_STATE)
    bm = jnp.repeat(bm, heads_per_group, axis=2)
    cm = jnp.repeat(cm, heads_per_group, axis=2)
    dt = jax.nn.softplus(dt_raw.astype(jnp.float32) + dt_bias.astype(jnp.float32))
    a = -jnp.exp(a_log.astype(jnp.float32))
    y = ssd_chunked(xs * dt[..., None], dt * a, bm, cm) + d_skip.astype(jnp.float32)[:, None] * xs
    y = y.reshape(b, T, D_INNER) * jax.nn.silu(z.astype(jnp.float32))
    y = y.reshape(b, T, D_GROUPS, D_INNER // D_GROUPS)
    y = y * lax.rsqrt(jnp.mean(jnp.square(y), axis=-1, keepdims=True) + D_NORM_EPS)
    return (y.reshape(b, T, D_INNER) * norm_w).astype(z.dtype)

def grouped_expert_ffn(x2d, expert, gate, w_gate, w_up, w_down):
    m, dm = x2d.shape
    n_assign = m * TOP_K_EXPERTS
    flat_e = expert.reshape(-1)
    flat_tok = jnp.arange(n_assign) // TOP_K_EXPERTS
    flat_gate = gate.reshape(-1)
    order = jnp.argsort(flat_e)
    se, stok, sgate = flat_e[order], flat_tok[order], flat_gate[order]
    counts = jnp.bincount(flat_e, length=N_EXPERTS)
    padded = (counts + MOE_BLOCK - 1) // MOE_BLOCK * MOE_BLOCK
    pad_end = jnp.cumsum(padded)
    pad_start = pad_end - padded
    start = jnp.cumsum(counts) - counts
    dest = pad_start[se] + jnp.arange(n_assign) - start[se]
    cap = (n_assign + N_EXPERTS * (MOE_BLOCK - 1) + MOE_BLOCK - 1) // MOE_BLOCK * MOE_BLOCK
    n_blocks = cap // MOE_BLOCK
    buf_tok = jnp.full((cap,), m, dtype=jnp.int32).at[dest].set(stok)
    x_ext = jnp.concatenate([x2d, jnp.zeros((1, dm), x2d.dtype)], axis=0)
    xb = x_ext[buf_tok].reshape(n_blocks, MOE_BLOCK, dm)
    blk_expert = jnp.minimum(jnp.searchsorted(pad_end, jnp.arange(n_blocks) * MOE_BLOCK, side='right'),
                             N_EXPERTS - 1)

    def expert_block(args):
        xblk, e = args
        h = jax.nn.silu(xblk @ w_gate[e]) * (xblk @ w_up[e])
        return h @ w_down[e]

    yb = lax.map(expert_block, (xb, blk_expert)).reshape(cap, dm)
    y = yb[dest] * sgate[:, None]
    return jnp.zeros_like(x2d).at[stok].add(y)

def hierarchical_moe(x2d, wg, bg, we, be, w_gate, w_up, w_down):
    m = x2d.shape[0]
    xf = x2d.astype(jnp.float32)
    p_group = jax.nn.softmax(xf @ wg.astype(jnp.float32) + bg.astype(jnp.float32), axis=-1)
    pg_top, g_sel = lax.top_k(p_group, 1)
    logits_e = (xf @ we.astype(jnp.float32) + be.astype(jnp.float32)).reshape(m, N_EXPERT_GROUPS, EXPERTS_PER_GROUP)
    logits_e = logits_e[jnp.arange(m), g_sel[:, 0]]
    pe_top, e_sel = lax.top_k(jax.nn.softmax(logits_e, axis=-1), TOP_K_EXPERTS)
    gate = pg_top * pe_top / jnp.sum(pe_top, axis=-1, keepdims=True)
    expert = g_sel * EXPERTS_PER_GROUP + e_sel
    return grouped_expert_ffn(x2d, expert, gate.astype(x2d.dtype), w_gate, w_up, w_down)

def second_inputs(seed: int = 0) -> dict:
    key = jax.random.key(seed)
    ks = iter(jax.random.split(key, 48))
    L = DEPTH_2

    def nrm(shape, scale):
        return jax.random.normal(next(ks), shape, jnp.float32) * scale

    def unif(shape, lo, hi):
        return jax.random.uniform(next(ks), shape, jnp.float32, minval=lo, maxval=hi)

    dt = jnp.exp(unif((L, D_HEADS), math.log(1e-3), math.log(1e-1)))
    return {
        'x': nrm((BATCH, SEQ, D_MODEL), 1.0),
        'w_in': nrm((L, D_MODEL, IN_WIDTH_2), D_MODEL ** -0.5),
        'c_mu': unif((L, C_IN), 0.0, 1.0),
        'c_w0': unif((L, C_WIDTH), -6.0, -1.0),
        'c_w2': nrm((L, C_LORA_W, C_WIDTH), 0.1),
        'c_a0': nrm((L, C_WIDTH), 0.1),
        'c_a2': nrm((L, C_LORA_A, C_WIDTH), C_LORA_A ** -0.5),
        'c_g2': nrm((L, C_LORA_G, C_WIDTH), C_LORA_G ** -0.5),
        'c_kk': 0.85 + nrm((L, C_WIDTH), 0.02),
        'c_ka': 1.0 + nrm((L, C_WIDTH), 0.02),
        'c_rk': nrm((L, C_HEADS, HEAD_DIM), 0.1),
        'c_gn_w': 1.0 + nrm((L, C_WIDTH), 0.02),
        'c_gn_b': nrm((L, C_WIDTH), 0.02),
        'c_v0': nrm((L - 1, C_WIDTH), 0.1),
        'c_v1': nrm((L - 1, C_WIDTH, C_LORA_V), C_WIDTH ** -0.5),
        'c_v2': nrm((L - 1, C_LORA_V, C_WIDTH), C_LORA_V ** -0.5),
        'd_conv_w': nrm((L, D_CONV, D_XBC), D_CONV ** -0.5),
        'd_conv_b': nrm((L, D_XBC), 0.02),
        'd_dt_bias': dt + jnp.log(-jnp.expm1(-dt)),
        'd_a_log': jnp.log(unif((L, D_HEADS), 1.0, 16.0)),
        'd_skip': 1.0 + nrm((L, D_HEADS), 0.02),
        'd_norm_w': 1.0 + nrm((L, D_INNER), 0.02),
        'w_branch': nrm((L, N_BRANCH, BRANCH_WIDTH, D_MODEL), BRANCH_WIDTH ** -0.5),
        'w_out': nrm((L, D_MODEL, D_MODEL), D_MODEL ** -0.5 * DEEPNORM_BETA),
        'ln1_g': 1.0 + nrm((L, D_MODEL), 0.02),
        'ln1_b': nrm((L, D_MODEL), 0.02),
        'r_group': nrm((L, D_MODEL, N_EXPERT_GROUPS), D_MODEL ** -0.5),
        'r_group_b': nrm((L, N_EXPERT_GROUPS), 0.01),
        'r_expert': nrm((L, D_MODEL, N_EXPERTS), D_MODEL ** -0.5),
        'r_expert_b': nrm((L, N_EXPERTS), 0.01),
        'e_gate': nrm((L, N_EXPERTS, D_MODEL, D_EXPERT), D_MODEL ** -0.5),
        'e_up': nrm((L, N_EXPERTS, D_MODEL, D_EXPERT), D_MODEL ** -0.5),
        'e_down': nrm((L, N_EXPERTS, D_EXPERT, D_MODEL), D_EXPERT ** -0.5 * DEEPNORM_BETA),
        'ln2_g': 1.0 + nrm((L, D_MODEL), 0.02),
        'ln2_b': nrm((L, D_MODEL), 0.02),
    }

def second_block(x, w_in, c_mu, c_w0, c_w2, c_a0, c_a2, c_g2, c_kk, c_ka, c_rk, c_gn_w, c_gn_b,
              c_v0, c_v1, c_v2, d_conv_w, d_conv_b, d_dt_bias, d_a_log, d_skip, d_norm_w,
              w_branch, w_out, ln1_g, ln1_b, r_group, r_group_b, r_expert, r_expert_b,
              e_gate, e_up, e_down, ln2_g, ln2_b):
    b, T, _ = x.shape
    v_first = None
    for l in range(DEPTH_2):
        seg, off = {}, 0
        for name, size in IN_SEGMENTS:
            seg[name] = x @ w_in[l, :, off:off + size]
            off += size

        a_qkv = seg['a_qkv'].reshape(b, T, 3, A_GROUPS, A_HEADS, HEAD_DIM)
        o_a = dilated_window_attention([a_qkv[:, :, 0, g] for g in range(A_GROUPS)],
                                       [a_qkv[:, :, 1, g] for g in range(A_GROUPS)],
                                       [a_qkv[:, :, 2, g] for g in range(A_GROUPS)])

        b_qkv = seg['b_qkv'].reshape(b, T, 3, B_HEADS, HEAD_DIM)
        o_b = indexer_sparse_attention(b_qkv[:, :, 0], b_qkv[:, :, 1], b_qkv[:, :, 2],
                                       seg['b_idx_q'].reshape(b, T, IDX_HEADS, IDX_DIM),
                                       seg['b_idx_k'], seg['b_idx_w'])

        v_lora = None if l == 0 else (c_v0[l - 1], c_v1[l - 1], c_v2[l - 1])
        o_c, v_c = rwkv7_time_mix(seg['c_in'], c_mu[l], c_w0[l], c_w2[l], c_a0[l], c_a2[l], c_g2[l],
                                  c_kk[l], c_ka[l], c_rk[l], c_gn_w[l], c_gn_b[l], v_first, v_lora)
        if l == 0:
            v_first = v_c

        o_d = mamba2_mixer(seg['d_z'], seg['d_xbc'], seg['d_dt'], d_conv_w[l], d_conv_b[l],
                           d_dt_bias[l], d_a_log[l], d_skip[l], d_norm_w[l])

        gates = jax.nn.sigmoid(seg['gates'].reshape(b, T, N_BRANCH, D_MODEL))
        merged = jnp.zeros_like(x)
        for n, o_n in enumerate((o_a, o_b, o_c, o_d)):
            merged = merged + gates[:, :, n] * (o_n @ w_branch[l, n])
        x = layer_norm(DEEPNORM_ALPHA * x + merged @ w_out[l], ln1_g[l], ln1_b[l])

        y = hierarchical_moe(x.reshape(b * T, D_MODEL), r_group[l], r_group_b[l], r_expert[l],
                             r_expert_b[l], e_gate[l], e_up[l], e_down[l])
        x = layer_norm(DEEPNORM_ALPHA * x + y.reshape(b, T, D_MODEL), ln2_g[l], ln2_b[l])
    return x


_first_inputs = second_inputs


def second_inputs(seed=0):
    import zlib

    import numpy as np

    out = dict(_first_inputs(seed))
    spreads = {}
    factors = {'c_w2': 8.0,
     'c_a0': 5.463,
     'c_kk': 200.0,
     'c_ka': 63.395,
     'c_gn_w': 127.014,
     'c_gn_b': 106.223,
     'd_conv_b': 6.56,
     'd_a_log': 24.448,
     'd_skip': 200.0,
     'd_norm_w': 67.453,
     'r_group_b': 18.981,
     'r_expert_b': 18.673,
     'ln2_g': 22.895,
     'ln2_b': 22.986,
     'd_dt_bias': 27.36}
    for name, (base, spread) in spreads.items():
        noise = np.random.default_rng([zlib.crc32(name.encode()), seed]).standard_normal(out[name].shape)
        drawn = base * np.exp(spread * noise) if base else spread * noise
        out[name] = jnp.asarray(drawn.astype(out[name].dtype))
    for name, factor in factors.items():
        out[name] = (out[name] * factor).astype(out[name].dtype)
    return out


_narrow_inputs = second_inputs


def second_inputs(seed=0):

    out = dict(_narrow_inputs(seed))
    wider = {'c_kk': 5.83,
     'c_ka': 3.1,
     'c_gn_w': 3.73,
     'c_gn_b': 4.2,
     'd_skip': 12.0,
     'd_norm_w': 3.54,
     'ln2_g': 3.2,
     'ln2_b': 3.2}
    for name, times in wider.items():
        mean = out[name].mean()
        out[name] = (mean + times * (out[name] - mean)).astype(out[name].dtype)
    return out


def setup_inputs(seed=0):
    out = dict(first_inputs(seed))
    for name, value in second_inputs(seed + 1).items():
        if name != "x":
            out[name + "_2"] = value
    return out


def reference(
    x, c, ctx, c_ctx, w_ada, b_ada, norm_mix_g, norm_ffn_g, w_in, gla_wg2_fw, gla_bg_fw,
    gla_wg2_bw, gla_bg_bw, gla_norm_g, sc_conv_w, sc_conv_b, na_rpb, w_out, ffn_w_up,
    ffn_conv_w, ffn_conv_b, ffn_w_down, final_norm_g, w_in_2, c_mu_2, c_w0_2, c_w2_2, c_a0_2,
    c_a2_2, c_g2_2, c_kk_2, c_ka_2, c_rk_2, c_gn_w_2, c_gn_b_2, c_v0_2, c_v1_2, c_v2_2,
    d_conv_w_2, d_conv_b_2, d_dt_bias_2, d_a_log_2, d_skip_2, d_norm_w_2, w_branch_2, w_out_2,
    ln1_g_2, ln1_b_2, r_group_2, r_group_b_2, r_expert_2, r_expert_b_2, e_gate_2, e_up_2,
    e_down_2, ln2_g_2, ln2_b_2,
):
    x = first_block(
        x, c, ctx, c_ctx, w_ada, b_ada, norm_mix_g, norm_ffn_g, w_in, gla_wg2_fw, gla_bg_fw,
        gla_wg2_bw, gla_bg_bw, gla_norm_g, sc_conv_w, sc_conv_b, na_rpb, w_out, ffn_w_up,
        ffn_conv_w, ffn_conv_b, ffn_w_down, final_norm_g,
    )
    return second_block(
        x, w_in_2, c_mu_2, c_w0_2, c_w2_2, c_a0_2, c_a2_2, c_g2_2, c_kk_2, c_ka_2, c_rk_2,
        c_gn_w_2, c_gn_b_2, c_v0_2, c_v1_2, c_v2_2, d_conv_w_2, d_conv_b_2, d_dt_bias_2,
        d_a_log_2, d_skip_2, d_norm_w_2, w_branch_2, w_out_2, ln1_g_2, ln1_b_2, r_group_2,
        r_group_b_2, r_expert_2, r_expert_b_2, e_gate_2, e_up_2, e_down_2, ln2_g_2, ln2_b_2,
    )


_drawn_inputs = setup_inputs


def setup_inputs(seed=0):
    import zlib

    import numpy as np

    out = dict(_drawn_inputs(seed))
    spreads = {}
    factors = {'gla_bg_fw': 8.0,
     'gla_bg_bw': 8.0,
     'gla_norm_g': 2.813,
     'sc_conv_b': 3.597,
     'na_rpb': 51.031,
     'ffn_conv_b': 2.854}
    for name, (base, spread) in spreads.items():
        noise = np.random.default_rng([zlib.crc32(name.encode()), seed]).standard_normal(out[name].shape)
        drawn = base * np.exp(spread * noise) if base else spread * noise
        out[name] = jnp.asarray(drawn.astype(out[name].dtype))
    for name, factor in factors.items():
        out[name] = (out[name] * factor).astype(out[name].dtype)
    return out
```

```python
from contextlib import ExitStack

import numpy as np

import concourse.bass as bass
from concourse import mybir

F32 = mybir.dt.float32
I32 = mybir.dt.int32
ALU = mybir.AluOpType
ACT = mybir.ActivationFunctionType
AX = mybir.AxisListType

P = 128
D = 1024
KT = D // P
LAT, CTX = 512, 256
TOK = LAT + CTX
NT = TOK // P
NTL = LAT // P
CH = 16
FFN = 2816
FT = FFN // P
EPS = 1e-6
NEG = -1e30
SLOT = 2048
NSLOT = 4


class Engine:

    def __init__(self, sem):
        self.sem, self.n, self.seen = sem, 0, {}

    def mark(self, ins):
        self.n += 1
        return (self.sem, self.n)

    def last(self):
        return (self.sem, self.n)

    def behind(self, ticket):
        sem, n = ticket
        if n <= self.seen.get(id(sem), 0):
            return False
        self.seen[id(sem)] = n
        return True


class Queue:

    def __init__(self, sem):
        self.sem, self.n = sem, 0

    def mark(self, ins):
        self.n += 16
        return (self.sem, self.n)


class Core:

    def __init__(self, nc, ctx):
        self.nc, self.ctx = nc, ctx
        sem = lambda n: ctx.enter_context(nc.semaphore(n))
        self.pe_done = sem("pe_done")
        self.pe = Engine(self.pe_done)
        self.act_done = sem("act_done")
        self.act = Engine(self.act_done)
        self.dve_done = sem("dve_done")
        self.dve = Engine(self.dve_done)
        self.pool_done = sem("pool_done")
        self.pool = Engine(self.pool_done)
        self.sp_done = sem("sp_done")
        self.sp = Engine(self.sp_done)
        self.loaded = [Queue(sem(f"slot{i}_loaded")) for i in range(NSLOT)]
        self.params = Queue(sem("params_loaded"))
        self.stored = Queue(sem("stored"))
        self.bank = [ctx.enter_context(nc.psum_tensor(f"bank{i}", [P, 512], F32)) for i in range(8)]
        self.bank_read = [[] for _ in range(8)]
        self.ring = ctx.enter_context(nc.sbuf_tensor("ring", [P, NSLOT, SLOT], F32))
        self.slot_used = [None] * NSLOT
        self.slot = 0
        self.turn = 0
        self.at_bank = -1

    def sb(self, name, shape):
        return self.ctx.enter_context(self.nc.sbuf_tensor(name, shape, F32))

    def fence(k):
        nc = k.nc
        marks = [e.last() for e in (k.pe, k.act, k.dve, k.pool) if e.n]
        for ticket in marks:
            if k.pe.behind(ticket):
                nc.tensor.wait_ge(*ticket)
        for ticket in marks:
            if k.act.behind(ticket):
                nc.scalar.wait_ge(*ticket)
        for ticket in marks:
            if k.dve.behind(ticket):
                nc.vector.wait_ge(*ticket)
        for ticket in marks:
            if k.pool.behind(ticket):
                nc.gpsimd.wait_ge(*ticket)

    def load(k, src, rows, cols):
        nc = k.nc
        s = k.slot
        k.slot = (s + 1) % NSLOT
        if k.slot_used[s]:
            if k.sp.behind(k.slot_used[s]):
                nc.sync.wait_ge(*k.slot_used[s])
        view = k.ring[:, s, 0:rows * cols].rearrange("p (r c) -> p r c", r=rows)
        t = k.loaded[s].mark(nc.sync.dma_start(view, src).then_inc(k.loaded[s].sem, 16))
        return view, t, s

    def free(k, s):
        k.slot_used[s] = k.pe.last()

    def next_bank(k, avoid=None, low=False):
        n = 4 if low else 8
        k.at_bank = (k.at_bank + 1) % n
        if k.at_bank == avoid:
            k.at_bank = (k.at_bank + 1) % n
        return k.at_bank

    def take(k, b):
        nc = k.nc
        for ticket in k.bank_read[b]:
            if k.pe.behind(ticket):
                nc.tensor.wait_ge(*ticket)
        k.bank_read[b] = []
        return k.bank[b]

    def evac(k, b, out, src, after, same=False):
        nc = k.nc
        k.turn += 0 if same else 1
        if k.turn % 2:
            if k.act.behind(after):
                nc.scalar.wait_ge(*after)
            t = k.act.mark(nc.scalar.copy(out, src).then_inc(k.act_done, 1))
        else:
            if k.dve.behind(after):
                nc.vector.wait_ge(*after)
            t = k.dve.mark(nc.vector.tensor_copy(out, src).then_inc(k.dve_done, 1))
        k.bank_read[b].append(t)
        return t


def matmuls(k, out, pairs):
    nc = k.nc
    n = len(pairs)
    for i, (w, x) in enumerate(pairs):
        ins = nc.tensor.matmul(out, w, x, start=(i == 0), stop=(i == n - 1))
    return k.pe.mark(ins.then_inc(k.pe_done, 1))


def project_features(k, w_dram, cols, xT, n_tok, tiles, ready):
    nc = k.nc
    kt = w_dram.shape[0] // P
    w, t_w, s = k.load(w_dram[:, cols[0]:cols[1]].rearrange("(t p) c -> p t c", p=P), kt, cols[1] - cols[0])
    if k.pe.behind(t_w):
        nc.tensor.wait_ge(*t_w)
    for ticket in ready:
        if k.pe.behind(ticket):
            nc.tensor.wait_ge(*ticket)
    for c, width, tok, epilogue in tiles:
        for t0 in range(tok[0], tok[1], 512):
            t1 = min(t0 + 512, tok[1])
            b = k.next_bank()
            ps = k.take(b)
            t = matmuls(k, ps[0:width, 0:t1 - t0],
                        [(w[:, i, c - cols[0]:c - cols[0] + width], xT[:, i, t0:t1]) for i in range(kt)])
            k.bank_read[b] += epilogue(ps[0:width, 0:t1 - t0], t0, t1, t)
    k.free(s)


def project_tokens(k, w_dram, cols, xT, tok_tiles, epilogue, ready):
    nc = k.nc
    kt = w_dram.shape[0] // P
    n = cols[1] - cols[0]
    w, t_w, s = k.load(w_dram[:, cols[0]:cols[1]].rearrange("(t p) c -> p t c", p=P), kt, n)
    if k.pe.behind(t_w):
        nc.tensor.wait_ge(*t_w)
    for ticket in ready:
        if k.pe.behind(ticket):
            nc.tensor.wait_ge(*ticket)
    for tt in tok_tiles:
        b = k.next_bank()
        ps = k.take(b)
        t = matmuls(k, ps[:, 0:n], [(xT[:, i, tt * P:(tt + 1) * P], w[:, i, :]) for i in range(kt)])
        k.bank_read[b] += epilogue(ps[:, 0:n], tt, t)
    k.free(s)


def copy_out(k, dst):
    nc = k.nc
    def epilogue(ps, *where):
        after = where[-1]
        k.turn += 1
        if k.turn % 2:
            if k.act.behind(after):
                nc.scalar.wait_ge(*after)
            return [k.act.mark(nc.scalar.copy(dst(*where[:-1]), ps).then_inc(k.act_done, 1))]
        if k.dve.behind(after):
            nc.vector.wait_ge(*after)
        return [k.dve.mark(nc.vector.tensor_copy(dst(*where[:-1]), ps).then_inc(k.dve_done, 1))]
    return epilogue



def features(v):
    v = np.asarray(v)
    lead = int(np.prod(v.shape[:-1], dtype=int))
    return np.ascontiguousarray(v.reshape(lead, v.shape[-1] // P, P).transpose(2, 0, 1).reshape(P, -1))


def rows(v):
    return np.asarray(v).reshape(1, -1)


def all_rows(v):
    return np.repeat(np.asarray(v).reshape(1, -1), P, 0)


def param_columns(i):
    cols = {}
    cols["cond"] = np.stack([features(i["c"][0]), features(i["c_ctx"])], -1).reshape(P, -1)
    for name in ("b_ada", "norm_mix_g", "norm_ffn_g", "sc_conv_w", "sc_conv_b", "ffn_conv_w", "ffn_conv_b"):
        cols[name] = features(i[name])
    cols["final_norm_g"] = features(i["final_norm_g"])
    cols["gla_norm_g"] = np.concatenate([i["gla_norm_g"].T] * 2, 0)
    gate = np.zeros((32, 2, 384), np.float32)
    gate[0:16, :, 0:192] = i["gla_wg2_fw"].transpose(1, 0, 2)
    gate[16:32, :, 192:384] = i["gla_wg2_bw"].transpose(1, 0, 2)
    cols["gla_wg2"] = gate.reshape(32, -1)
    cols["gla_bg"] = rows(np.concatenate([i["gla_bg_fw"], i["gla_bg_bw"]], 1))
    for name in ("c_mu", "c_w0", "c_a0", "c_kk", "c_ka", "c_gn_w", "c_gn_b", "d_conv_w", "d_conv_b",
                 "d_norm_w", "ln1_g", "ln1_b", "ln2_g", "ln2_b"):
        cols[name] = features(i[name + "_2"])
    cols["c_rk"] = features(i["c_rk_2"].reshape(1, 256))
    cols["c_lora"] = np.concatenate([i["c_w2_2"][0], i["c_a2_2"][0], i["c_g2_2"][0]], 0)
    cols["d_skip"] = features(np.repeat(i["d_skip_2"].reshape(1, 4), 64, 1))
    cols["d_dt_bias"] = all_rows(i["d_dt_bias_2"])
    cols["d_a_log"] = all_rows(i["d_a_log_2"])
    cols["router_b"] = all_rows(np.concatenate([i["r_group_b_2"], i["r_expert_b_2"]], 1))
    router = np.concatenate([i["r_group_2"][0], i["r_expert_2"][0]], 1)
    cols["router_w"] = router.reshape(KT, P, 36).transpose(1, 0, 2).reshape(P, -1)
    return cols


def const_columns():
    j = np.arange(P)[:, None]
    i = np.arange(P)[None, :]
    same = j // CH == i // CH
    cols = {}
    cols["ident"] = j == i
    cols["ones"] = np.ones((P, P))
    cols["upto"] = same & (j <= i)
    cols["from"] = same & (j >= i)
    cols["after"] = same & (j > i)
    cols["before"] = same & (j < i)
    cols["tri"] = j <= i
    cols["tri_after"] = j > i
    cols["tri_before"] = j < i
    cols["halves"] = j // 64 == i // 64
    cols["chunk_of"] = j // CH == np.arange(P // CH)[None, :]
    cols["eps"] = np.tile([[EPS, 1e-5, 64e-5, 0.0]], (P, 1))
    inv = (np.float32(10000.0) ** (-np.arange(8, dtype=np.float32) / np.float32(8))).astype(np.float32)
    t = np.arange(LAT)
    ang = np.concatenate([(t // 64)[:, None].astype(np.float32) * inv, (t % 64)[:, None].astype(np.float32) * inv], 1)
    for name, f in (("cos", np.cos), ("sin", np.sin)):
        cols[name] = f(ang).astype(np.float32).reshape(NTL, P, 16).transpose(1, 0, 2).reshape(P, -1)
    cols["iota"] = np.tile(np.arange(P)[None, :], (P, 1))
    cols["expert"] = np.tile(np.arange(32)[None, :], (P, 1))
    return cols


def dilated_masks():
    q = np.arange(P)[:, None]
    back = q - np.arange(-384, P)[None, :]
    m = [np.where((back >= 0) & (back <= win) & (back % dil == 0), 0.0, NEG) for win, dil in ((128, 1), (512, 4), (2048, 16))]
    return np.stack(m, 1).reshape(P, -1)


def pack(cols):
    where, at = {}, 0
    for name, a in cols.items():
        where[name] = (at, a.shape[0], a.shape[1])
        at += a.shape[1]
    out = np.zeros((P, at), np.float32)
    for name, a in cols.items():
        f, r, n = where[name]
        out[0:r, f:f + n] = a
    return out, where



class State:
    pass


def repeat(v, n):
    return v.rearrange("p (a c) -> p a c", a=1).to_broadcast([v.shape[0], n, v.shape[-1]])


def sum_partitions(k, s, weights, src, n, tiles, ready):
    nc = k.nc
    out = []
    for t0 in range(0, n, 512):
        t1 = min(t0 + 512, n)
        b = k.next_bank()
        ps = k.take(b)
        for ticket in ready:
            if k.pe.behind(ticket):
                nc.tensor.wait_ge(*ticket)
        out.append((b, ps[:, 0:t1 - t0], t0, t1, matmuls(k, ps[:, 0:t1 - t0], [(weights, src[:, i, t0:t1]) for i in tiles])))
    return out


def inverse_root(k, s, dst, parts, scale, eps):
    nc = k.nc
    for b, ps, t0, t1, t in parts:
        if k.act.behind(t):
            nc.scalar.wait_ge(*t)
        r = k.act.mark(k.nc.scalar.activation(dst[:, t0:t1], ps, ACT.Sqrt, bias=eps, scale=scale).then_inc(k.act_done, 1))
        k.bank_read[b].append(r)
        if k.dve.behind(r):
            nc.vector.wait_ge(*r)
        k.dve.mark(k.nc.vector.reciprocal(dst[:, t0:t1], dst[:, t0:t1]).then_inc(k.dve_done, 1))
    return k.dve.last()


def rms_norm(k, s, xT, n, out, gain, shift, split):
    nc = k.nc
    k.fence()
    for i in range(KT):
        sq = k.act.mark(nc.scalar.activation(out[:, i, 0:n], xT[:, i, 0:n], ACT.Square).then_inc(k.act_done, 1))
    parts = sum_partitions(k, s, s.c("ones"), out, n, range(KT), [sq])
    rs = inverse_root(k, s, s.rstd, parts, 1.0 / D, s.c("eps")[:, 0:1])
    if k.dve.behind(rs):
        nc.vector.wait_ge(*rs)
    groups = [(0, 0, LAT)] + ([(1, LAT, n)] if n > LAT else [])
    for i in range(KT):
        for g, t0, t1 in groups:
            k.dve.mark(nc.vector.scalar_tensor_tensor(out[:, i, t0:t1], xT[:, i, t0:t1], gain(i, g),
                                                      s.rstd[:, t0:t1], ALU.mult, ALU.mult).then_inc(k.dve_done, 1))
        if shift is not None:
            if k.act.behind(k.dve.last()):
                nc.scalar.wait_ge(*k.dve.last())
            for g, t0, t1 in groups:
                k.act.mark(nc.scalar.activation(out[:, i, t0:t1], out[:, i, t0:t1], ACT.Identity,
                                                bias=shift(i, g)).then_inc(k.act_done, 1))
    return [k.act.last(), k.dve.last()]


def modulation(k, s, layer):
    nc = k.nc
    k.fence()
    w_dram = s.d["w_ada"][layer]
    b = k.next_bank()
    ps = k.take(b)
    for g in range(24):
        w, t_w, slot = k.load(w_dram[:, g * 256:(g + 1) * 256].rearrange("(t p) c -> p t c", p=P), KT, 256)
        if k.pe.behind(t_w):
            nc.tensor.wait_ge(*t_w)
        if k.pe.behind(s.cond_ready):
            nc.tensor.wait_ge(*s.cond_ready)
        for m in range(2):
            o = (2 * g + m) * 2
            t = matmuls(k, ps[:, o:o + 2], [(w[:, i, m * P:(m + 1) * P], s.cond[:, i, :]) for i in range(KT)])
        k.free(slot)
    if k.dve.behind(t):
        nc.vector.wait_ge(*t)
    bias = s.p("b_ada")[:, layer * 48:(layer + 1) * 48]
    psv = ps[:, 0:96].rearrange("p (m g) -> p m g", g=2)
    for g in range(2):
        t = k.dve.mark(nc.vector.tensor_tensor(s.mod[:, :, g], psv[:, :, g], bias, ALU.add).then_inc(k.dve_done, 1))
    k.bank_read[b].append(t)
    if k.dve.behind(t):
        nc.vector.wait_ge(*t)
    for which, name in ((0, "norm_mix_g"), (1, "norm_ffn_g")):
        gain = s.p(name)[:, layer * KT:(layer + 1) * KT]
        for g in range(2):
            k.dve.mark(nc.vector.scalar_tensor_tensor(
                s.gains[:, which, :, g], s.mod[:, 8 + 24 * which:16 + 24 * which, g], 1.0, gain, ALU.add, ALU.mult).then_inc(k.dve_done, 1))
    if k.act.behind(k.dve.last()):
        nc.scalar.wait_ge(*k.dve.last())


def gated_linear_attention(k, s, layer, hT, h_ready, with_ctx):
    nc = k.nc
    w_in = s.d["w_in"][layer]
    k.fence()
    A = s.arena
    mark = A.mark()
    tok = A.take([NT, 768])
    ke = A.take([NT, 384])
    qdT = A.take([4, TOK])
    kiT = A.take([4, TOK])
    states = A.take([2, TOK // CH, 64])
    over = states.rearrange("p a b c -> p (a b c)")
    g = over[:, 0:NT * 384].rearrange("p (t c) -> p t c", t=NT)
    glrT = over[0:32, NT * 384:NT * 384 + TOK]
    tail = s.mix[:, 3:8, :].rearrange("p a b -> p (a b)")
    tmp = tail[:, 0:4 * 768].rearrange("p (a b) -> p a b", a=4)
    dec = s.small[:, 0:4 * 48].rearrange("p (a b) -> p a b", a=4)

    for c in range(0, 768, 256):
        project_tokens(k, w_in, (c, c + 256), hT, range(NT), copy_out(k, lambda tt, c=c: tok[:, tt, c:c + 256]), h_ready)
    project_features(k, w_in, (768, 800), hT, TOK,
                     [(768, 32, (0, TOK), copy_out(k, lambda t0, t1: glrT[:, t0:t1]))], h_ready)
    k.fence()

    wg2 = s.p("gla_wg2")[:, layer * 384:(layer + 1) * 384]
    bg = s.p("gla_bg")[:, layer * 384:(layer + 1) * 384]
    for tt in range(NT):
        b = k.next_bank()
        ps = k.take(b)
        t = matmuls(k, ps[:, 0:384], [(glrT[:, tt * P:(tt + 1) * P], wg2), (s.c("ones")[0:1, :], bg)])
        if k.dve.behind(t):
            nc.vector.wait_ge(*t)
        x = tmp[:, tt % 4, 0:384]
        if tt >= 4:
            if k.dve.behind(logs[tt - 4]):
                nc.vector.wait_ge(*logs[tt - 4])
        logs = [] if tt == 0 else logs
        if k.act.behind(t):
            nc.scalar.wait_ge(*t)
        if tt >= 4:
            if k.act.behind(k.dve.last()):
                nc.scalar.wait_ge(*k.dve.last())
        t3 = k.act.mark(nc.scalar.activation(x, ps[:, 0:384], ACT.Abs).then_inc(k.act_done, 1))
        nc.scalar.wait_ge(*k.act.last())
        if k.dve.behind(t3):
            nc.vector.wait_ge(*t3)
        t2 = k.dve.mark(nc.vector.tensor_scalar(g[:, tt, :], ps[:, 0:384], 0.0, None, ALU.min).then_inc(k.dve_done, 1))
        k.bank_read[b] += [t2]
        k.act.mark(nc.scalar.activation(x, x, ACT.Exp, scale=-1.0).then_inc(k.act_done, 1))
        nc.scalar.wait_ge(*k.act.last())
        logs.append(k.act.mark(nc.scalar.activation(x, x, ACT.Ln, bias=1.0).then_inc(k.act_done, 1)))
        if k.dve.behind(t2):
            nc.vector.wait_ge(*t2)
        if k.dve.behind(logs[-1]):
            nc.vector.wait_ge(*logs[-1])
        k.dve.mark(nc.vector.tensor_tensor(g[:, tt, :], g[:, tt, :], x, ALU.subtract).then_inc(k.dve_done, 1))
    k.fence()

    for tt in range(NTL):
        qk = tok[:, tt, 0:384].rearrange("p (h f two) -> p h f two", h=12, two=2)
        cos = s.c("cos")[:, tt * 16:(tt + 1) * 16].rearrange("p (a f) -> p a f", a=1).to_broadcast([P, 12, 16])
        sin = s.c("sin")[:, tt * 16:(tt + 1) * 16].rearrange("p (a f) -> p a f", a=1).to_broadcast([P, 12, 16])
        a, bb, c, d = (tmp[:, i, 0:192].rearrange("p (h f) -> p h f", h=12) for i in range(4))
        k.dve.mark(nc.vector.tensor_tensor(a, qk[:, :, :, 0], cos, ALU.mult).then_inc(k.dve_done, 1))
        k.dve.mark(nc.vector.tensor_tensor(bb, qk[:, :, :, 1], sin, ALU.mult).then_inc(k.dve_done, 1))
        k.dve.mark(nc.vector.tensor_tensor(c, qk[:, :, :, 0], sin, ALU.mult).then_inc(k.dve_done, 1))
        k.dve.mark(nc.vector.tensor_tensor(d, qk[:, :, :, 1], cos, ALU.mult).then_inc(k.dve_done, 1))
        nc.vector.wait_ge(*k.dve.last())
        k.dve.mark(nc.vector.tensor_tensor(qk[:, :, :, 0], a, bb, ALU.subtract).then_inc(k.dve_done, 1))
        k.dve.mark(nc.vector.tensor_tensor(qk[:, :, :, 1], c, d, ALU.add).then_inc(k.dve_done, 1))
        nc.vector.wait_ge(*k.dve.last())

    k.fence()
    bd = k.next_bank()
    psd = k.take(bd)
    for tt in range(NT):
        gf, gb = g[:, tt, 0:192], g[:, tt, 192:384]
        b1 = k.next_bank(avoid=bd)
        ps = k.take(b1)
        matmuls(k, ps[:, 0:192], [(s.c("upto"), gf)])
        tb = matmuls(k, ps[:, 192:384], [(s.c("from"), gb)])
        b2 = k.next_bank(avoid=bd)
        ps2 = k.take(b2)
        matmuls(k, ps2[:, 0:192], [(s.c("after"), gf)])
        te = matmuls(k, ps2[:, 192:384], [(s.c("before"), gb)])
        for j, (f, m) in enumerate(((0, 128), (192, 128), (128, 64), (320, 64))):
            td = matmuls(k, psd[0:m, j * 48 + tt * 8:j * 48 + tt * 8 + 8], [(g[:, tt, f:f + m], s.c("chunk_of"))])
        eb, en, qd, ki = (tmp[:, i, 0:384] for i in range(4))
        if k.act.behind(tb):
            nc.scalar.wait_ge(*tb)
        if k.act.behind(k.dve.last()):
            nc.scalar.wait_ge(*k.dve.last())
        k.act.mark(nc.scalar.activation(eb, ps[:, 0:384], ACT.Exp, scale=1 / 16).then_inc(k.act_done, 1))
        t1 = k.act.mark(nc.scalar.activation(en, ps[:, 0:384], ACT.Exp, scale=-1 / 16).then_inc(k.act_done, 1))
        k.bank_read[b1].append(t1)
        if k.act.behind(te):
            nc.scalar.wait_ge(*te)
        t2 = k.act.mark(nc.scalar.activation(ke[:, tt, :], ps2[:, 0:384], ACT.Exp, scale=1 / 16).then_inc(k.act_done, 1))
        k.bank_read[b2].append(t2)
        if k.dve.behind(t2):
            nc.vector.wait_ge(*t2)
        if k.dve.behind(k.pe.last()):
            nc.vector.wait_ge(*k.pe.last())
        two = lambda v: v.rearrange("p (d c) -> p d c", d=2)
        q2 = tok[:, tt, 0:192].rearrange("p (a c) -> p a c", a=1).to_broadcast([P, 2, 192])
        k2 = tok[:, tt, 192:384].rearrange("p (a c) -> p a c", a=1).to_broadcast([P, 2, 192])
        k.dve.mark(nc.vector.scalar_tensor_tensor(two(qd), two(eb), 32 ** -0.5, q2, ALU.mult, ALU.mult).then_inc(k.dve_done, 1))
        k.dve.mark(nc.vector.tensor_tensor(two(ki), two(en), k2, ALU.mult).then_inc(k.dve_done, 1))
        t3 = k.dve.mark(nc.vector.tensor_tensor(two(ke[:, tt, :]), two(ke[:, tt, :]), k2, ALU.mult).then_inc(k.dve_done, 1))
        for src, dst in ((qd, qdT), (ki, kiT)):
            b3 = k.next_bank(avoid=bd)
            ps3 = k.take(b3)
            if k.pe.behind(t3):
                nc.tensor.wait_ge(*t3)
            for j, (f, m) in enumerate(((0, 128), (192, 128), (128, 64), (320, 64))):
                t4 = k.pe.mark(nc.tensor.transpose(ps3[0:m, j * P:(j + 1) * P], src[:, f:f + m], s.c("ident")).then_inc(k.pe_done, 1))
            view = ps3[:, 0:512].rearrange("p (a c) -> p a c", a=4)
            k.evac(b3, dst[:, 0:2, tt * P:(tt + 1) * P], view[:, 0:2, :], t4)
            k.evac(b3, dst[0:64, 2:4, tt * P:(tt + 1) * P], view[0:64, 2:4, :], t4, same=True)
        if k.dve.behind(k.pe.last()):
            nc.vector.wait_ge(*k.pe.last())
    if k.act.behind(td):
        nc.scalar.wait_ge(*td)
    psdv = psd[:, 0:192].rearrange("p (a c) -> p a c", a=4)
    k.act.mark(nc.scalar.activation(dec[:, 0:2, :], psdv[:, 0:2, :], ACT.Exp, scale=1 / 16).then_inc(k.act_done, 1))
    t = k.act.mark(nc.scalar.activation(dec[0:64, 2:4, :], psdv[0:64, 2:4, :], ACT.Exp, scale=1 / 16).then_inc(k.act_done, 1))
    k.bank_read[bd].append(t)
    k.fence()

    ve = tail[:, 0:4 * 512].rearrange("p (a c v) -> p a c v", a=4, c=8)
    at = tail[:, 2048:2048 + 2 * 512].rearrange("p (a c) -> p a c", a=2)
    chunk = s.c("chunk_of").rearrange("p (c a) -> p c a", a=1).to_broadcast([P, 8, 64])
    order = {0: list(range(32, 48)) + list(range(0, 32)), 1: list(range(47, 31, -1)) + list(range(31, -1, -1))}
    for ht, heads in ((0, (0, 1, 2, 3)), (1, (4, 5))):
        rows_ = 32 * len(heads)
        chain = [None, None]
        used = {}
        for d in range(2):
            chain[d] = k.dve.mark(nc.vector.memset(states[0:rows_, d, order[d][0], :], 0.0).then_inc(k.dve_done, 1))
        for step in range(6):
            kv = {}
            for d in range(2):
                tt = order[d][step * 8] // 8
                b = d * 2 + step % 2
                ps = k.take(b)
                for h in heads:
                    i = (h + d * 2) % 4 if len(heads) == 2 else h
                    if i in used:
                        if k.pool.behind(used[i]):
                            nc.gpsimd.wait_ge(*used[i])
                    v3 = tok[:, tt, 384 + 64 * h:448 + 64 * h].rearrange("p (a v) -> p a v", a=1).to_broadcast([P, 8, 64])
                    tv = k.pool.mark(nc.gpsimd.tensor_tensor(ve[:, i], v3, chunk, ALU.mult).then_inc(k.pool_done, 1))
                    if k.pe.behind(tv):
                        nc.tensor.wait_ge(*tv)
                    o = 32 * (h - heads[0])
                    t = matmuls(k, ps[o:o + 32, :], [(ke[:, tt, d * 192 + 32 * h:d * 192 + 32 * h + 32],
                                                      ve[:, i].rearrange("p c v -> p (c v)"))])
                    used[i] = t
                kv[d] = (b, ps, t)
            for j in range(8):
                for d in range(2):
                    n = order[d][step * 8 + j]
                    b, ps, t = kv[d]
                    if step * 8 + j + 1 < 48:
                        nxt = order[d][step * 8 + j + 1]
                        if k.dve.behind(t):
                            nc.vector.wait_ge(*t)
                        if k.dve.behind(chain[d]):
                            nc.vector.wait_ge(*chain[d])
                        c = n % 8
                        chain[d] = k.dve.mark(nc.vector.scalar_tensor_tensor(
                            states[0:rows_, d, nxt, :], states[0:rows_, d, n, :], dec[0:rows_, 2 * ht + d, n:n + 1],
                            ps[0:rows_, c * 64:(c + 1) * 64], ALU.mult, ALU.add).then_inc(k.dve_done, 1))
            for d in range(2):
                k.bank_read[kv[d][0]].append(k.dve.last())
        k.fence()
        for h in heads:
            o = 32 * (h - heads[0])
            groups = [(0, 0, 4)] + ([(1, 4, 6)] if with_ctx else [])
            for gi, ta, tb_ in groups:
                n_tok = (tb_ - ta) * P
                bo = 4 + (h % 2) * 2 + gi
                po = k.take(bo)
                first = True
                for d in range(2):
                    bs = k.next_bank(low=True)
                    ps = k.take(bs)
                    for tt in range(ta, tb_):
                        cols = slice(tt * P, (tt + 1) * P)
                        t = matmuls(k, ps[:, (tt - ta) * P:(tt - ta + 1) * P],
                                    [(kiT[o:o + 32, 2 * ht + d, cols], qdT[o:o + 32, 2 * ht + d, cols])])
                    if k.dve.behind(t):
                        nc.vector.wait_ge(*t)
                    if s.at_used[d]:
                        if k.dve.behind(s.at_used[d]):
                            nc.vector.wait_ge(*s.at_used[d])
                    t = k.dve.mark(nc.vector.tensor_tensor(
                        at[:, d, 0:n_tok].rearrange("p (a c) -> p a c", c=P), ps[:, 0:n_tok].rearrange("p (a c) -> p a c", c=P),
                        repeat(s.c(("upto", "from")[d]), tb_ - ta), ALU.mult).then_inc(k.dve_done, 1))
                    k.bank_read[bs].append(t)
                    for n in range(ta * 8, tb_ * 8):
                        tc_ = (n - ta * 8) * CH
                        nc.tensor.matmul(po[0:64, tc_:tc_ + CH], states[o:o + 32, d, n, :],
                                         qdT[o:o + 32, 2 * ht + d, n * CH:(n + 1) * CH],
                                         start=first, stop=False, skip_group_check=True)
                        first = False
                    if k.pe.behind(t):
                        nc.tensor.wait_ge(*t)
                    for tt in range(ta, tb_):
                        c0 = (tt - ta) * P
                        ins = nc.tensor.matmul(po[0:64, c0:c0 + P], tok[:, tt, 384 + 64 * h:448 + 64 * h],
                                               at[:, d, c0:c0 + P], start=False,
                                               stop=(d == 1 and tt == tb_ - 1), skip_group_check=True)
                    s.at_used[d] = k.pe.mark(ins.then_inc(k.pe_done, 1))
                k.evac(bo, s.mix[64 * (h % 2):64 * (h % 2) + 64, h // 2, ta * P:tb_ * P], po[0:64, 0:n_tok], s.at_used[1])
    k.fence()
    A.reset(mark)

    n = TOK if with_ctx else LAT
    r = A.take([3, TOK])
    sq = A.take([3, TOK])
    rs = A.take([TOK])
    def silu_out(dst):
        def epilogue(ps, t0, t1, t):
            if k.act.behind(t):
                nc.scalar.wait_ge(*t)
            return [k.act.mark(nc.scalar.activation(dst[:, t0:t1], ps, ACT.Silu).then_inc(k.act_done, 1))]
        return epilogue
    project_features(k, w_in, (800, 1056), hT, TOK, [(800, P, (0, n), silu_out(r[:, 0])), (928, P, (0, n), silu_out(r[:, 1]))], [])
    project_features(k, w_in, (1056, 1184), hT, TOK, [(1056, P, (0, n), silu_out(r[:, 2]))], [])
    for i in range(3):
        if k.act.behind(k.dve.last()):
            nc.scalar.wait_ge(*k.dve.last())
        if k.act.behind(k.pe.last()):
            nc.scalar.wait_ge(*k.pe.last())
        t = k.act.mark(nc.scalar.activation(sq[:, i, 0:n], s.mix[:, i, 0:n], ACT.Square).then_inc(k.act_done, 1))
        parts = sum_partitions(k, s, s.c("halves"), sq, n, [i], [t])
        if k.act.behind(k.dve.last()):
            nc.scalar.wait_ge(*k.dve.last())
        inverse_root(k, s, rs, parts, 1.0 / 64, s.c("eps")[:, 0:1])
        if k.dve.behind(k.dve.last()):
            nc.vector.wait_ge(*k.dve.last())
        if k.dve.behind(k.act.last()):
            nc.vector.wait_ge(*k.act.last())
        k.dve.mark(nc.vector.scalar_tensor_tensor(s.mix[:, i, 0:n], s.mix[:, i, 0:n], s.p("gla_norm_g")[:, layer:layer + 1],
                                                  rs[:, 0:n], ALU.mult, ALU.mult).then_inc(k.dve_done, 1))
        nc.vector.wait_ge(*k.dve.last())
        k.dve.mark(nc.vector.tensor_tensor(s.mix[:, i, 0:n], s.mix[:, i, 0:n], r[:, i, 0:n], ALU.mult).then_inc(k.dve_done, 1))
    A.reset(mark)


def short_convolution(k, s, layer, hT, n):
    nc = k.nc
    w_in = s.d["w_in"][layer]
    k.fence()
    A = s.arena
    mark = A.mark()
    b = A.take([2, TOK])
    c = A.take([2, TOK])
    y = A.take([2, TOK])
    for j, dst in enumerate((b, c, y)):
        c0 = 1184 + 256 * j
        project_features(k, w_in, (c0, c0 + 256), hT, TOK,
                         [(c0 + P * m, P, (0, n), copy_out(k, lambda t0, t1, m=m, dst=dst: dst[:, m, t0:t1])) for m in range(2)], [])
    k.fence()
    w = lambda tap, m: s.p("sc_conv_w")[:, (layer * 3 + tap) * 2 + m:(layer * 3 + tap) * 2 + m + 1]
    spans = [(0, LAT)] + ([(LAT, n)] if n > LAT else [])
    k.dve.mark(nc.vector.tensor_tensor(c[:, :, 0:n], c[:, :, 0:n], y[:, :, 0:n], ALU.mult).then_inc(k.dve_done, 1))
    nc.vector.wait_ge(*k.dve.last())
    for m in range(2):
        k.dve.mark(nc.vector.tensor_scalar(y[:, m, 0:n], c[:, m, 0:n], w(1, m), s.p("sc_conv_b")[:, layer * 2 + m:layer * 2 + m + 1], ALU.mult, ALU.add).then_inc(k.dve_done, 1))
        nc.vector.wait_ge(*k.dve.last())
        for t0, t1 in spans:
            k.dve.mark(nc.vector.scalar_tensor_tensor(y[:, m, t0 + 1:t1], c[:, m, t0:t1 - 1], w(0, m), y[:, m, t0 + 1:t1], ALU.mult, ALU.add).then_inc(k.dve_done, 1))
            nc.vector.wait_ge(*k.dve.last())
            k.dve.mark(nc.vector.scalar_tensor_tensor(y[:, m, t0:t1 - 1], c[:, m, t0 + 1:t1], w(2, m), y[:, m, t0:t1 - 1], ALU.mult, ALU.add).then_inc(k.dve_done, 1))
            nc.vector.wait_ge(*k.dve.last())
    k.dve.mark(nc.vector.tensor_tensor(s.mix[:, 3:5, 0:n], b[:, :, 0:n], y[:, :, 0:n], ALU.mult).then_inc(k.dve_done, 1))
    k.fence()
    A.reset(mark)


def attention(k, s, jobs, scale):
    nc = k.nc
    A = s.arena
    mark = A.mark()
    wide = 1536
    scores = A.take([2, wide])
    turned = A.take([2, 512])
    stat = s.small[:, 200:208]
    k.fence()
    pv_done = [None, None]
    turned_used = [None, None]
    n_turn = [0]

    def softmax(j):
        segments, out = jobs[j]
        e = j % 2
        at = 0
        if pv_done[e]:
            if k.dve.behind(pv_done[e]):
                nc.vector.wait_ge(*pv_done[e])
        spans = []
        for i, (qT, kT, bias, values, ready) in enumerate(segments):
            width = kT.shape[-1]
            b = 3 * e + i
            ps = k.take(b)
            if ready:
                for ticket in ready:
                    if k.pe.behind(ticket):
                        nc.tensor.wait_ge(*ticket)
                for ticket in ready:
                    if k.dve.behind(ticket):
                        nc.vector.wait_ge(*ticket)
            t = matmuls(k, ps[:, 0:width], [(qT, kT)])
            if k.dve.behind(t):
                nc.vector.wait_ge(*t)
            dst = scores[:, e, at:at + width]
            if bias is None:
                t = k.dve.mark(nc.vector.tensor_scalar(dst, ps[:, 0:width], scale, None, ALU.mult).then_inc(k.dve_done, 1))
            else:
                t = k.dve.mark(nc.vector.scalar_tensor_tensor(dst, ps[:, 0:width], scale, bias, ALU.mult, ALU.add).then_inc(k.dve_done, 1))
            k.bank_read[b].append(t)
            spans.append((at, width, values))
            at += width
        if k.dve.behind(k.dve.last()):
            nc.vector.wait_ge(*k.dve.last())
        p = scores[:, e, 0:at]
        k.dve.mark(nc.vector.reduce_max(stat[:, e:e + 1], p, AX.X).then_inc(k.dve_done, 1))
        nc.vector.wait_ge(*k.dve.last())
        k.dve.mark(nc.vector.tensor_scalar(stat[:, 2 + e:3 + e], stat[:, e:e + 1], -1.0, None, ALU.mult).then_inc(k.dve_done, 1))
        if k.act.behind(k.dve.last()):
            nc.scalar.wait_ge(*k.dve.last())
        k.act.mark(nc.scalar.activation(p, p, ACT.Exp, bias=stat[:, 2 + e:3 + e], accum_out=stat[:, 4 + e:5 + e]).then_inc(k.act_done, 1))
        if k.dve.behind(k.act.last()):
            nc.vector.wait_ge(*k.act.last())
        k.dve.mark(nc.vector.reciprocal(stat[:, 6 + e:7 + e], stat[:, 4 + e:5 + e]).then_inc(k.dve_done, 1))
        nc.vector.wait_ge(*k.dve.last())
        t = k.dve.mark(nc.vector.tensor_scalar(p, p, stat[:, 6 + e:7 + e], None, ALU.mult).then_inc(k.dve_done, 1))
        return spans, t

    def weighted_sum(j, spans, t_p):
        e = j % 2
        out = jobs[j][1]
        tiles = [(at + P * i, values[i]) for at, width, values in spans for i in range(width // P)]
        po = k.take(7)
        for i0 in range(0, len(tiles), 4):
            part = tiles[i0:i0 + 4]
            ps = k.take(6)
            if k.pe.behind(t_p):
                nc.tensor.wait_ge(*t_p)
            for i, (at, _) in enumerate(part):
                t = k.pe.mark(nc.tensor.transpose(ps[:, i * P:(i + 1) * P], scores[:, e, at:at + P], s.c("ident")).then_inc(k.pe_done, 1))
            u = n_turn[0] % 2
            n_turn[0] += 1
            if turned_used[u]:
                if k.act.behind(turned_used[u]):
                    nc.scalar.wait_ge(*turned_used[u])
            if k.act.behind(t):
                nc.scalar.wait_ge(*t)
            t = k.act.mark(nc.scalar.copy(turned[:, u, 0:P * len(part)], ps[:, 0:P * len(part)]).then_inc(k.act_done, 1))
            k.bank_read[6].append(t)
            if k.pe.behind(t):
                nc.tensor.wait_ge(*t)
            for i, (_, v) in enumerate(part):
                ins = nc.tensor.matmul(po[0:64, 0:P], v, turned[:, u, i * P:(i + 1) * P],
                                       start=(i0 + i == 0), stop=(i0 + i == len(tiles) - 1))
            turned_used[u] = k.pe.mark(ins.then_inc(k.pe_done, 1))
        pv_done[e] = turned_used[u]
        if k.act.behind(pv_done[e]):
            nc.scalar.wait_ge(*pv_done[e])
        k.bank_read[7].append(k.act.mark(nc.scalar.copy(out, po[0:64, 0:P]).then_inc(k.act_done, 1)))
        if s.after_job:
            s.after_job(j)

    ahead = softmax(0)
    for j in range(len(jobs)):
        nxt = softmax(j + 1) if j + 1 < len(jobs) else None
        weighted_sum(j, *ahead)
        ahead = nxt
    k.fence()
    A.reset(mark)


def local_and_context_attention(k, s, layer, hT, with_ctx):
    nc = k.nc
    w_in = s.d["w_in"][layer]
    A = s.arena
    mark = A.mark()
    q = A.take([3, TOK])
    kk = A.take([3, TOK])
    v = A.take([NT, 384])
    bias = A.take([2, NTL, 512])
    nq = TOK if with_ctx else LAT
    for base, dst, n in ((1952, q, nq), (2336, kk, TOK)):
        for c0, w in ((0, 256), (256, 128)):
            project_features(k, w_in, (base + c0, base + c0 + w), hT, TOK,
                             [(base + c0 + P * m, P, (0, n), copy_out(k, lambda t0, t1, i=c0 // P + m, dst=dst: dst[:, i, t0:t1]))
                              for m in range(w // P)], [])
    for c0, w in ((0, 256), (256, 128)):
        project_tokens(k, w_in, (2720 + c0, 2720 + c0 + w), hT, range(NT), copy_out(k, lambda tt, c0=c0, w=w: v[:, tt, c0:c0 + w]), [])
    k.fence()
    jobs = []
    bias_ready = {}
    rpb = s.d["rpb"][layer]

    def load_bias(h):
        q_ = Queue(s.bias_loaded[h % 2])
        q_.n = s.bias_count[h % 2]
        for r in range(8):
            src = rpb[h, :, 7 - r:15 - r, :].rearrange("q i c -> q (i c)")
            bias_ready[h] = q_.mark(nc.gpsimd.dma_start(bias[64 * (r % 2):64 * (r % 2) + 64, h % 2, r // 2, :], src).then_inc(q_.sem, 16))
        s.bias_count[h % 2] = q_.n

    def ctx_values(h):
        return [v[:, 4 + i, 64 * h:64 * h + 64] for i in range(2)]

    if k.pool.behind(k.dve.last()):
        nc.gpsimd.wait_ge(*k.dve.last())
    load_bias(0)
    load_bias(1)
    for h in range(6):
        o = 64 * (h % 2)
        hq, hk = q[o:o + 64, h // 2, :], kk[o:o + 64, h // 2, :]
        for i in range(NTL):
            qT = hq[:, i * P:(i + 1) * P]
            jobs.append(([(qT, hk[:, 0:LAT], bias[:, h % 2, i, :], [v[:, tt, 64 * h:64 * h + 64] for tt in range(4)],
                           ("bias", h)),
                          (qT, hk[:, LAT:TOK], None, ctx_values(h), None)],
                         s.mix[o:o + 64, 5 + h // 2, i * P:(i + 1) * P]))
    if with_ctx:
        for h in range(6):
            o = 64 * (h % 2)
            hq, hk = q[o:o + 64, h // 2, :], kk[o:o + 64, h // 2, :]
            for i in range(4, 6):
                jobs.append(([(hq[:, i * P:(i + 1) * P], hk[:, LAT:TOK], None, ctx_values(h), None)],
                             s.mix[o:o + 64, 5 + h // 2, i * P:(i + 1) * P]))

    class Ready(dict):
        pass

    resolved = []
    for segs, out in jobs:
        resolved.append((segs, out))

    def fill(j):
        if j % NTL == NTL - 1 and j // NTL + 2 < 6 and j < 24:
            if k.pool.behind(k.dve.last()):
                nc.gpsimd.wait_ge(*k.dve.last())
            load_bias(j // NTL + 2)
    s.after_job = fill

    class Jobs(list):
        def __getitem__(self, j):
            segs, out = list.__getitem__(self, j)
            return ([(a, b_, c, d, [bias_ready[r[1]]] if r else None) for a, b_, c, d, r in segs], out)
    attention(k, s, Jobs(resolved), 64 ** -0.5)
    s.after_job = None
    A.reset(mark)


def output_projection(k, s, w_dram, xin, n, gate):
    nc = k.nc
    k.fence()
    for c0 in range(0, D, 256):
        tiles = []
        for m in range(2):
            mt = c0 // P + m

            def residual(ps, t0, t1, t, mt=mt):
                if k.dve.behind(t):
                    nc.vector.wait_ge(*t)
                return [k.dve.mark(nc.vector.scalar_tensor_tensor(s.xT[:, mt, t0:t1], ps, gate(mt, t0 // LAT),
                                                                  s.xT[:, mt, t0:t1], ALU.mult, ALU.add).then_inc(k.dve_done, 1))]
            tiles.append((c0 + m * P, P, (0, n), residual))
        project_features(k, w_dram, (c0, c0 + 256), xin, n, tiles, [])


def conv_ffn(k, s, layer, hT, n):
    nc = k.nc
    A = s.arena
    mark = A.mark()
    k.fence()
    A.reset(0)
    act = A.take([FT, TOK])
    raw = A.take([4, TOK])
    con = A.take([4, TOK])
    up = s.d["ffn_w_up"][layer]
    spans = [(0, LAT)] + ([(LAT, n)] if n > LAT else [])
    w = lambda tap, m: s.p("ffn_conv_w")[:, (layer * 3 + tap) * 44 + m:(layer * 3 + tap) * 44 + m + 1]
    bias = lambda m: s.p("ffn_conv_b")[:, layer * 44 + m:layer * 44 + m + 1]
    raw_free = [None] * 4
    con_free = [None] * 4

    for g in range(FT // 2):
        for half in range(2):
            c0 = half * FFN + g * 256
            loaded = k.load(up[:, c0:c0 + 256].rearrange("(t p) c -> p t c", p=P), KT, 256)
            if k.pe.behind(loaded[1]):
                nc.tensor.wait_ge(*loaded[1])
            for m in range(2):
                mt = c0 // P + m
                i = half * 2 + m
                done = []
                for t0, t1 in spans:
                    b = k.next_bank()
                    ps = k.take(b)
                    t = matmuls(k, ps[:, 0:t1 - t0], [(loaded[0][:, kt, m * P:(m + 1) * P], hT[:, kt, t0:t1]) for kt in range(KT)])
                    if k.act.behind(t):
                        nc.scalar.wait_ge(*t)
                    if raw_free[i]:
                        if k.act.behind(raw_free[i]):
                            nc.scalar.wait_ge(*raw_free[i])
                    if con_free[i]:
                        if k.act.behind(con_free[i]):
                            nc.scalar.wait_ge(*con_free[i])
                    k.act.mark(nc.scalar.copy(raw[:, i, t0:t1], ps[:, 0:t1 - t0]).then_inc(k.act_done, 1))
                    ta = k.act.mark(nc.scalar.activation(con[:, i, t0:t1], ps[:, 0:t1 - t0], ACT.Identity, bias=bias(mt), scale=w(1, mt)).then_inc(k.act_done, 1))
                    k.bank_read[b].append(ta)
                    if k.dve.behind(ta):
                        nc.vector.wait_ge(*ta)
                    k.dve.mark(nc.vector.scalar_tensor_tensor(con[:, i, t0 + 1:t1], raw[:, i, t0:t1 - 1], w(0, mt), con[:, i, t0 + 1:t1], ALU.mult, ALU.add).then_inc(k.dve_done, 1))
                    nc.vector.wait_ge(*k.dve.last())
                    raw_free[i] = k.dve.mark(nc.vector.scalar_tensor_tensor(con[:, i, t0:t1 - 1], raw[:, i, t0 + 1:t1], w(2, mt), con[:, i, t0:t1 - 1], ALU.mult, ALU.add).then_inc(k.dve_done, 1))
                if half == 0:
                    if k.act.behind(raw_free[i]):
                        nc.scalar.wait_ge(*raw_free[i])
                    con_free[i] = k.act.mark(nc.scalar.activation(con[:, i, 0:n], con[:, i, 0:n], ACT.Silu).then_inc(k.act_done, 1))
                else:
                    if k.dve.behind(k.act.last()):
                        nc.vector.wait_ge(*k.act.last())
                    if k.dve.behind(raw_free[i]):
                        nc.vector.wait_ge(*raw_free[i])
                    con_free[i] = con_free[m] = k.dve.mark(nc.vector.tensor_tensor(act[:, 2 * g + m, 0:n], con[:, m, 0:n], con[:, i, 0:n], ALU.mult).then_inc(k.dve_done, 1))
            k.free(loaded[2])
    k.fence()
    down = s.d["ffn_w_down"][layer]
    for mt in range(KT):
        banks = []
        for t0, t1 in spans:
            b = k.next_bank()
            banks.append((b, k.take(b)))
        for half in range(2):
            r0 = half * 11 * P
            w_, t_w, slot = k.load(down[r0:r0 + 11 * P, mt * P:(mt + 1) * P].rearrange("(t p) c -> p t c", p=P), 11, P)
            if k.pe.behind(t_w):
                nc.tensor.wait_ge(*t_w)
            for (b, ps), (t0, t1) in zip(banks, spans):
                for i in range(11):
                    ins = nc.tensor.matmul(ps[:, 0:t1 - t0], w_[:, i, :], act[:, half * 11 + i, t0:t1],
                                           start=(half == 0 and i == 0), stop=(half == 1 and i == 10))
                t = k.pe.mark(ins.then_inc(k.pe_done, 1))
            k.free(slot)
        if k.dve.behind(t):
            nc.vector.wait_ge(*t)
        for g, ((b, ps), (t0, t1)) in enumerate(zip(banks, spans)):
            k.bank_read[b].append(k.dve.mark(nc.vector.scalar_tensor_tensor(
                s.xT[:, mt, t0:t1], ps[:, 0:t1 - t0], s.mod[:, 40 + mt, g:g + 1], s.xT[:, mt, t0:t1], ALU.mult, ALU.add).then_inc(k.dve_done, 1)))
    k.fence()
    A.reset(mark)


def first_block(k, s, layers=2):
    nc = k.nc
    for layer in range(layers):
        with_ctx = layer == 0
        n = TOK if with_ctx else LAT
        modulation(k, s, layer)
        ready = rms_norm(k, s, s.xT, TOK, s.hT, lambda i, g: s.gains[:, 0, i, g:g + 1], lambda i, g: s.mod[:, i, g:g + 1], True)
        gated_linear_attention(k, s, layer, s.hT, ready, with_ctx)
        short_convolution(k, s, layer, s.hT, n)
        local_and_context_attention(k, s, layer, s.hT, with_ctx)
        output_projection(k, s, s.d["w_out"][layer], s.mix, n, lambda m, g: s.mod[:, 16 + m, g:g + 1])
        ready = rms_norm(k, s, s.xT, n, s.hT, lambda i, g: s.gains[:, 1, i, g:g + 1], lambda i, g: s.mod[:, 24 + i, g:g + 1], True)
        k.fence()
        conv_ffn(k, s, layer, s.hT, n)
    rms_norm(k, s, s.xT, LAT, s.hT, lambda i, g: s.p("final_norm_g")[:, i:i + 1], None, False)
    k.fence()



SEG = {}
_at = 0
for _name, _n in (("a_q", 768), ("a_k", 768), ("a_v", 768), ("b_q", 256), ("b_k", 256), ("b_v", 256), ("idx_q", 256),
                  ("idx_k", 64), ("idx_w", 4), ("c_in", 896), ("d_z", 256), ("d_xbc", 512), ("d_dt", 4),
                  ("gates", 4096)):
    SEG[_name] = _at
    _at += _n
ALPHA = 2 ** 0.25
N_EXP, PER_GROUP, D_EXP = 32, 8, 512


def into_features(k, s, name, n, dst):
    for c0 in range(0, n, 256):
        w = min(256, n - c0)
        first = SEG[name] + c0
        project_features(k, s.d["w_in_2"], (first, first + w), s.hT, LAT,
                         [(first + P * m, min(P, w), (0, LAT), copy_out(k, lambda t0, t1, i=c0 // P + m: dst[:, i, :]))
                          for m in range(w // P)], [])


def into_tokens(k, s, name, n, dst):
    for c0 in range(0, n, 256):
        w = min(256, n - c0)
        first = SEG[name] + c0
        project_tokens(k, s.d["w_in_2"], (first, first + w), s.hT, range(NTL),
                       copy_out(k, lambda tt, c0=c0, w=w: dst[:, tt, c0:c0 + w]), [])


def dilated_attention(k, s):
    nc = k.nc
    A = s.arena
    mark = A.mark()
    q = A.take([6, LAT])
    kk = A.take([6, LAT])
    v = A.take([NTL, 768])
    masks = A.take([3, 512])
    k.fence()
    t = k.params.mark(nc.scalar.dma_start(masks.rearrange("p a b -> p (a b)"), s.d["dilated_masks"]).then_inc(k.params.sem, 16))
    into_features(k, s, "a_q", 768, q)
    into_features(k, s, "a_k", 768, kk)
    into_tokens(k, s, "a_v", 768, v)
    k.fence()
    if k.dve.behind(t):
        nc.vector.wait_ge(*t)
    jobs = []
    for h in range(4):
        o = 64 * (h % 2)
        for i in range(NTL):
            segs = []
            for g in range(3):
                j0 = max(0, i - 1) if g == 0 else 0
                tile = 2 * g + h // 2
                segs.append((q[o:o + 64, tile, i * P:(i + 1) * P], kk[o:o + 64, tile, j0 * P:(i + 1) * P],
                             masks[:, g, (3 - i + j0) * P:512],
                             [v[:, j, 256 * g + 64 * h:256 * g + 64 * h + 64] for j in range(j0, i + 1)], None))
            jobs.append((segs, s.branch[o:o + 64, h // 2, i * P:(i + 1) * P]))
    attention(k, s, jobs, 64 ** -0.5)
    A.reset(mark)


def indexed_attention(k, s):
    nc = k.nc
    A = s.arena
    mark = A.mark()
    q = A.take([2, LAT])
    kk = A.take([2, LAT])
    v = A.take([NTL, 256])
    iq = A.take([2, LAT])
    ik = A.take([LAT])
    iw = A.take([NTL, 4])
    bias = A.take([NTL, 512])
    relu = A.take([2, 512])
    top = A.take([NTL, 8])
    k.fence()
    into_features(k, s, "b_q", 256, q)
    into_features(k, s, "b_k", 256, kk)
    into_tokens(k, s, "b_v", 256, v)
    into_features(k, s, "idx_q", 256, iq)

    def both_halves(ps, t0, t1, t):
        if k.act.behind(t):
            nc.scalar.wait_ge(*t)
        k.act.mark(nc.scalar.copy(ik[0:64, :], ps).then_inc(k.act_done, 1))
        return [k.act.mark(nc.scalar.copy(ik[64:128, :], ps).then_inc(k.act_done, 1))]
    f = SEG["idx_k"]
    project_features(k, s.d["w_in_2"], (f, f + 64), s.hT, LAT, [(f, 64, (0, LAT), both_halves)], [])
    into_tokens(k, s, "idx_w", 4, iw)
    k.fence()
    used = [None, None]
    for i in range(NTL):
        n = (i + 1) * P
        for h in range(4):
            o = 64 * (h % 2)
            b = k.next_bank()
            ps = k.take(b)
            t = matmuls(k, ps[:, 0:n], [(iq[o:o + 64, h // 2, i * P:(i + 1) * P], ik[o:o + 64, 0:n])])
            if k.act.behind(t):
                nc.scalar.wait_ge(*t)
            if used[h % 2]:
                if k.act.behind(used[h % 2]):
                    nc.scalar.wait_ge(*used[h % 2])
            t = k.act.mark(nc.scalar.activation(relu[:, h % 2, 0:n], ps[:, 0:n], ACT.Relu).then_inc(k.act_done, 1))
            k.bank_read[b].append(t)
            if k.dve.behind(t):
                nc.vector.wait_ge(*t)
            if k.dve.behind(k.dve.last()):
                nc.vector.wait_ge(*k.dve.last())
            if h == 0:
                t = k.dve.mark(nc.vector.tensor_scalar(bias[:, i, 0:n], relu[:, 0, 0:n], iw[:, i, 0:1], None, ALU.mult).then_inc(k.dve_done, 1))
            else:
                t = k.dve.mark(nc.vector.scalar_tensor_tensor(bias[:, i, 0:n], relu[:, h % 2, 0:n], iw[:, i, h:h + 1],
                                                              bias[:, i, 0:n], ALU.mult, ALU.add).then_inc(k.dve_done, 1))
            used[h % 2] = t
        if k.pool.behind(t):
            nc.gpsimd.wait_ge(*t)
        k.pool.mark(nc.gpsimd.affine_select(out=bias[:, i, i * P:n], in_=bias[:, i, i * P:n], compare_op=ALU.is_ge,
                                            fill=NEG, base=0, pattern=[[-1, P]], channel_multiplier=1).then_inc(k.pool_done, 1))
    if k.dve.behind(k.pool.last()):
        nc.vector.wait_ge(*k.pool.last())
    last = {i: k.pool.last() for i in range(1, NTL)}
    for r in range(P // 8):
        for i in range(1, NTL):
            n = (i + 1) * P
            if k.dve.behind(last[i]):
                nc.vector.wait_ge(*last[i])
            last[i] = k.dve.mark(nc.vector.max(top[:, i, :], bias[:, i, 0:n]).then_inc(k.dve_done, 1))
        for i in range(1, NTL):
            n = (i + 1) * P
            if k.dve.behind(last[i]):
                nc.vector.wait_ge(*last[i])
            last[i] = k.dve.mark(nc.vector.match_replace(out=bias[:, i, 0:n], in_to_replace=top[:, i, :],
                                                         in_values=bias[:, i, 0:n], imm_value=-3e38).then_inc(k.dve_done, 1))
    for ticket in last.values():
        if k.dve.behind(ticket):
            nc.vector.wait_ge(*ticket)
    k.dve.mark(nc.vector.tensor_scalar(bias[:, 0, 0:P], bias[:, 0, 0:P], -1e29, NEG, ALU.is_lt, ALU.mult).then_inc(k.dve_done, 1))
    for i in range(1, NTL):
        n = (i + 1) * P
        k.dve.mark(nc.vector.tensor_scalar(bias[:, i, 0:n], bias[:, i, 0:n], -2e38, NEG, ALU.is_gt, ALU.mult).then_inc(k.dve_done, 1))
    if k.dve.behind(k.dve.last()):
        nc.vector.wait_ge(*k.dve.last())
    jobs = []
    for h in range(4):
        o = 64 * (h % 2)
        for i in range(NTL):
            n = (i + 1) * P
            jobs.append(([(q[o:o + 64, h // 2, i * P:n], kk[o:o + 64, h // 2, 0:n], bias[:, i, 0:n],
                           [v[:, j, 64 * h:64 * h + 64] for j in range(i + 1)], None)],
                         s.branch[o:o + 64, 2 + h // 2, i * P:(i + 1) * P]))
    attention(k, s, jobs, 64 ** -0.5)
    A.reset(mark)


def rwkv_mixer(k, s):
    nc = k.nc
    A = s.arena
    mark = A.mark()
    pc = A.take([7, LAT])
    d = A.take([2, LAT])
    k.fence()
    into_features(k, s, "c_in", 768, pc)
    f = SEG["c_in"] + 768
    project_features(k, s.d["w_in_2"], (f, f + P), s.hT, LAT, [(f, P, (0, LAT), copy_out(k, lambda t0, t1: pc[:, 6, :]))], [])
    k.fence()
    for i in range(7):
        e = i % 2
        k.dve.mark(nc.vector.tensor_tensor(d[:, e, 1:LAT], pc[:, i, 0:LAT - 1], pc[:, i, 1:LAT], ALU.subtract).then_inc(k.dve_done, 1))
        k.dve.mark(nc.vector.tensor_scalar(d[:, e, 0:1], pc[:, i, 0:1], -1.0, None, ALU.mult).then_inc(k.dve_done, 1))
        nc.vector.wait_ge(*k.dve.last())
        k.dve.mark(nc.vector.scalar_tensor_tensor(pc[:, i, :], d[:, e, :], s.p("c_mu")[:, i:i + 1], pc[:, i, :], ALU.mult, ALU.add).then_inc(k.dve_done, 1))
    k.fence()
    k.act.mark(nc.scalar.activation(pc[0:32, 6, :], pc[0:32, 6, :], ACT.Tanh).then_inc(k.act_done, 1))
    k.act.mark(nc.scalar.activation(pc[64:128, 6, :], pc[64:128, 6, :], ACT.Sigmoid).then_inc(k.act_done, 1))
    if k.pe.behind(k.act.last()):
        nc.tensor.wait_ge(*k.act.last())
    body = A.mark()
    for m in range(2):
        rwkv_pair(k, s, pc, m)
        A.reset(body)
    A.reset(mark)


def rwkv_pair(k, s, pc, m):
    nc = k.nc
    A = s.arena
    k.fence()
    r, key, v = pc[:, m, :], pc[:, 2 + m, :], pc[:, 4 + m, :]
    par = lambda n: s.p(n)[:, m:m + 1]
    lora = s.p("c_lora")[:, m * P:(m + 1) * P]
    ld, a, gate, kk, kmod, beta = (A.take([LAT]) for _ in range(6))
    alpha, kappa, rho, beta_e, kappa_e, rp = (A.take([LAT]) for _ in range(6))
    e1, e2 = A.take([LAT]), A.take([LAT])
    v_tok, be_tok, ke_tok, ld_tok = (A.take([NTL, P]) for _ in range(4))
    wx = A.take([NTL, 2, P])
    wu = A.take([NTL, P])
    MT = A.take([32, 64])
    N = A.take([32, 64])
    S = A.take([33, 64])
    mats = [A.take([NTL * P]) for _ in range(8)]
    g_end = s.small[:, 0:32]

    for o, n, dst in ((0, 32, ld), (32, 32, a), (64, 64, gate)):
        b = k.next_bank()
        ps = k.take(b)
        t = matmuls(k, ps[:, :], [(lora[o:o + n, :], pc[o:o + n, 6, :])])
        if k.act.behind(t):
            nc.scalar.wait_ge(*t)
        if dst is gate:
            t = k.act.mark(nc.scalar.copy(dst, ps[:, :]).then_inc(k.act_done, 1))
        else:
            t = k.act.mark(nc.scalar.activation(dst, ps[:, :], ACT.Sigmoid, bias=par("c_w0" if dst is ld else "c_a0")).then_inc(k.act_done, 1))
        k.bank_read[b].append(t)
    if k.dve.behind(k.act.last()):
        nc.vector.wait_ge(*k.act.last())
    k.dve.mark(nc.vector.tensor_scalar(ld, ld, -float(np.exp(-0.5)), None, ALU.mult).then_inc(k.dve_done, 1))
    k.dve.mark(nc.vector.tensor_scalar(kk, key, par("c_kk"), None, ALU.mult).then_inc(k.dve_done, 1))
    nc.vector.wait_ge(*k.dve.last())
    k.dve.mark(nc.vector.tensor_tensor(e1, kk, kk, ALU.mult).then_inc(k.dve_done, 1))
    nc.vector.wait_ge(*k.dve.last())
    b = k.next_bank()
    ps = k.take(b)
    if k.pe.behind(k.dve.last()):
        nc.tensor.wait_ge(*k.dve.last())
    t = matmuls(k, ps[:, :], [(s.c("halves"), e1)])
    if k.act.behind(t):
        nc.scalar.wait_ge(*t)
    t = k.act.mark(nc.scalar.activation(e2, ps[:, :], ACT.Sqrt).then_inc(k.act_done, 1))
    k.bank_read[b].append(t)
    if k.dve.behind(t):
        nc.vector.wait_ge(*t)
    k.dve.mark(nc.vector.tensor_scalar(e2, e2, 1e-12, None, ALU.max).then_inc(k.dve_done, 1))
    nc.vector.wait_ge(*k.dve.last())
    k.dve.mark(nc.vector.reciprocal(e2, e2).then_inc(k.dve_done, 1))
    nc.vector.wait_ge(*k.dve.last())
    k.dve.mark(nc.vector.tensor_tensor(kk, kk, e2, ALU.mult).then_inc(k.dve_done, 1))
    nc.vector.wait_ge(*k.dve.last())
    k.dve.mark(nc.vector.tensor_scalar(e1, a, -1.0, par("c_ka"), ALU.add, ALU.mult).then_inc(k.dve_done, 1))
    nc.vector.wait_ge(*k.dve.last())
    k.dve.mark(nc.vector.scalar_tensor_tensor(kmod, e1, 1.0, key, ALU.add, ALU.mult).then_inc(k.dve_done, 1))
    k.dve.mark(nc.vector.tensor_tensor(a, kk, a, ALU.mult).then_inc(k.dve_done, 1))
    nc.vector.wait_ge(*k.dve.last())
    if k.pe.behind(k.dve.last()):
        nc.tensor.wait_ge(*k.dve.last())
    if k.act.behind(k.dve.last()):
        nc.scalar.wait_ge(*k.dve.last())
    turn4(k, s, ld, ld_tok)
    turn4(k, s, v, v_tok)
    if k.pe.behind(k.act.last()):
        nc.tensor.wait_ge(*k.act.last())
    if k.pe.behind(k.dve.last()):
        nc.tensor.wait_ge(*k.dve.last())

    def decays(mask):
        b = k.next_bank()
        ps = k.take(b)
        for tt in range(NTL):
            t = matmuls(k, ps[:, tt * P:(tt + 1) * P], [(ld_tok[:, tt, :], s.c(mask))])
        if k.act.behind(t):
            nc.scalar.wait_ge(*t)
        if k.act.behind(k.dve.last()):
            nc.scalar.wait_ge(*k.dve.last())
        return b, ps
    b, ps = decays("upto")
    k.act.mark(nc.scalar.activation(e1, ps[:, :], ACT.Exp).then_inc(k.act_done, 1))
    k.bank_read[b].append(k.act.mark(nc.scalar.activation(e2, ps[:, :], ACT.Exp, scale=-1.0).then_inc(k.act_done, 1)))
    if k.dve.behind(k.act.last()):
        nc.vector.wait_ge(*k.act.last())
    k.dve.mark(nc.vector.tensor_tensor(rho, r, e1, ALU.mult).then_inc(k.dve_done, 1))
    k.dve.mark(nc.vector.tensor_tensor(beta, a, e2, ALU.mult).then_inc(k.dve_done, 1))
    k.dve.mark(nc.vector.tensor_tensor(kappa, kmod, e2, ALU.mult).then_inc(k.dve_done, 1))
    b, ps = decays("before")
    k.act.mark(nc.scalar.activation(e1, ps[:, :], ACT.Exp).then_inc(k.act_done, 1))
    b2, ps2 = decays("after")
    t = k.act.mark(nc.scalar.activation(e2, ps2[:, :], ACT.Exp).then_inc(k.act_done, 1))
    k.bank_read[b].append(t)
    k.bank_read[b2].append(t)
    if k.dve.behind(t):
        nc.vector.wait_ge(*t)
    k.dve.mark(nc.vector.scalar_tensor_tensor(alpha, kk, -1.0, e1, ALU.mult, ALU.mult).then_inc(k.dve_done, 1))
    k.dve.mark(nc.vector.tensor_tensor(beta_e, a, e2, ALU.mult).then_inc(k.dve_done, 1))
    k.dve.mark(nc.vector.tensor_tensor(kappa_e, kmod, e2, ALU.mult).then_inc(k.dve_done, 1))
    b = k.next_bank()
    ps = k.take(b)
    for tt in range(NTL):
        t = matmuls(k, ps[:, tt * 8:tt * 8 + 8], [(ld_tok[:, tt, :], s.c("chunk_of"))])
    if k.act.behind(t):
        nc.scalar.wait_ge(*t)
    k.bank_read[b].append(k.act.mark(nc.scalar.activation(g_end, ps[:, 0:32], ACT.Exp).then_inc(k.act_done, 1)))
    if k.pe.behind(k.dve.last()):
        nc.tensor.wait_ge(*k.dve.last())
    turn4(k, s, beta_e, be_tok)
    turn4(k, s, kappa_e, ke_tok)
    turn4(k, s, alpha, ke_tok, dst2=[wx[:, :, hh, 0:64] for hh in range(2)])
    k.fence()

    def products(lhs, rhs, dst, mask, plus_ident=False):
        b = k.next_bank(low=True)
        ps = k.take(b)
        for tt in range(NTL):
            c = slice(tt * P, (tt + 1) * P)
            t = matmuls(k, ps[:, c], [(lhs[:, c], rhs[:, c])])
        if k.dve.behind(t):
            nc.vector.wait_ge(*t)
        four = lambda x: x.rearrange("p (a c) -> p a c", c=P)
        if mask:
            t = k.dve.mark(nc.vector.tensor_tensor(four(dst), four(ps[:, 0:512]), repeat(s.c(mask), NTL), ALU.mult).then_inc(k.dve_done, 1))
        elif plus_ident:
            t = k.dve.mark(nc.vector.tensor_tensor(dst, ps[:, :], dst, ALU.add).then_inc(k.dve_done, 1))
        else:
            if k.act.behind(t):
                nc.scalar.wait_ge(*t)
            t = k.act.mark(nc.scalar.copy(dst, ps[:, :]).then_inc(k.act_done, 1))
        k.bank_read[b].append(t)
        if k.pe.behind(t):
            nc.tensor.wait_ge(*t)
        return t

    for hh in range(2):
        o = 64 * hh
        rows_ = slice(o, o + 64)
        al, be, ka, rh = (x[rows_] for x in (alpha, beta, kappa, rho))
        Am, B, A2, B2, T, akT, rbT, rkT = mats
        k.fence()
        products(al, be, Am, "after")
        products(be, al, B, "before")
        products(ka, al, akT, "before")
        products(be, rh, rbT, "upto")
        products(ka, rh, rkT, "upto")
        four = lambda x: x.rearrange("p (a c) -> p a c", c=P)
        if k.dve.behind(k.dve.last()):
            nc.vector.wait_ge(*k.dve.last())
        t = k.dve.mark(nc.vector.tensor_tensor(four(T), four(B), repeat(s.c("ident"), NTL), ALU.add).then_inc(k.dve_done, 1))
        products(B, Am, A2, None)
        products(Am, B, B2, None)
        if k.pe.behind(t):
            nc.tensor.wait_ge(*t)
        products(A2, T, T, None, True)
        products(B2, A2, Am, None)
        products(A2, B2, B, None)
        products(Am, T, T, None, True)
        products(B, Am, A2, None)
        products(A2, T, T, None, True)
        b = k.next_bank(low=True)
        ps = k.take(b)
        for tt in range(NTL):
            t = matmuls(k, ps[:, tt * 64:(tt + 1) * 64], [(akT[:, tt * P:(tt + 1) * P], v_tok[:, tt, rows_])])
        if k.dve.behind(t):
            nc.vector.wait_ge(*t)
        t = k.dve.mark(nc.vector.tensor_copy(wx[:, :, hh, 64:128], ps[:, 0:256].rearrange("p (a c) -> p a c", a=NTL)).then_inc(k.dve_done, 1))
        k.bank_read[b].append(t)
        if k.pe.behind(t):
            nc.tensor.wait_ge(*t)
        b = k.next_bank(low=True)
        ps = k.take(b)
        for tt in range(NTL):
            t = matmuls(k, ps[:, tt * P:(tt + 1) * P], [(T[:, tt * P:(tt + 1) * P], wx[:, tt, hh, :])])
        if k.dve.behind(t):
            nc.vector.wait_ge(*t)
        t = k.dve.mark(nc.vector.tensor_copy(wu[:, :, :], ps[:, 0:512].rearrange("p (a c) -> p a c", a=NTL)).then_inc(k.dve_done, 1))
        k.bank_read[b].append(t)
        if k.pe.behind(t):
            nc.tensor.wait_ge(*t)
        b = k.next_bank(low=True)
        ps = k.take(b)
        for tt in range(NTL):
            c = slice(tt * P, (tt + 1) * P)
            t = matmuls(k, ps[rows_, c], [(wu[:, tt, 0:64], rbT[:, c])])
        if k.dve.behind(t):
            nc.vector.wait_ge(*t)
        t = k.dve.mark(nc.vector.tensor_tensor(rp[rows_], ps[rows_, :], rh, ALU.add).then_inc(k.dve_done, 1))
        k.bank_read[b].append(t)
        po = k.take(4 + hh)
        for tt in range(NTL):
            c = slice(tt * P, (tt + 1) * P)
            nc.tensor.matmul(po[rows_, c], wu[:, tt, 64:128], rbT[:, c], start=(tt == 0), stop=False, skip_group_check=True)
            k.pe.mark(nc.tensor.matmul(po[rows_, c], v_tok[:, tt, rows_], rkT[:, c], start=False, stop=False, skip_group_check=True).then_inc(k.pe_done, 1))
        for tt in range(NTL):
            spread = [mats[i] for i in (0, 1, 2)]
            if tt >= 1:
                if k.pool.behind(k.pe.last()):
                    nc.gpsimd.wait_ge(*k.pe.last())
            else:
                if k.pool.behind(k.pe.last()):
                    nc.gpsimd.wait_ge(*k.pe.last())
                if k.pool.behind(k.dve.last()):
                    nc.gpsimd.wait_ge(*k.dve.last())
                if k.pool.behind(k.act.last()):
                    nc.gpsimd.wait_ge(*k.act.last())
            for src, dst in ((be_tok[:, tt, rows_], spread[0]), (wu[:, tt, 64:128], spread[1]), (v_tok[:, tt, rows_], spread[2])):
                chunk = s.c("chunk_of").rearrange("p (c a) -> p c a", a=1).to_broadcast([P, 8, 64])
                t = k.pool.mark(nc.gpsimd.tensor_tensor(dst.rearrange("p (c v) -> p c v", c=8), repeat(src, 8), chunk, ALU.mult).then_inc(k.pool_done, 1))
            if k.pe.behind(t):
                nc.tensor.wait_ge(*t)
            b = k.next_bank(low=True)
            ps = k.take(b)
            t = matmuls(k, ps[rows_, :], [(wu[:, tt, 0:64], spread[0])])
            if k.dve.behind(t):
                nc.vector.wait_ge(*t)
            for c in range(8):
                n = tt * 8 + c
                t = k.dve.mark(nc.vector.scalar_tensor_tensor(
                    MT[rows_, n, :], s.c("ident")[rows_, o:o + 64], g_end[rows_, n:n + 1],
                    ps[rows_, c * 64:(c + 1) * 64], ALU.mult, ALU.add).then_inc(k.dve_done, 1))
            k.bank_read[b].append(t)
            b = k.next_bank(low=True)
            ps = k.take(b)
            t = matmuls(k, ps[rows_, :], [(be_tok[:, tt, rows_], spread[1]), (ke_tok[:, tt, rows_], spread[2])])
            if k.act.behind(t):
                nc.scalar.wait_ge(*t)
            k.bank_read[b].append(k.act.mark(nc.scalar.copy(N[rows_, tt * 8:tt * 8 + 8, :], ps[rows_, :].rearrange("p (c v) -> p c v", c=8)).then_inc(k.act_done, 1)))
    k.fence()
    last = [k.dve.mark(nc.vector.memset(S[:, 0, :], 0.0).then_inc(k.dve_done, 1))] * 2
    for n in range(32):
        for hh in range(2):
            rows_ = slice(64 * hh, 64 * hh + 64)
            if k.pe.behind(last[hh]):
                nc.tensor.wait_ge(*last[hh])
            nc.tensor.matmul(k.bank[4 + hh][rows_, n * CH:(n + 1) * CH], S[rows_, n, :], rp[rows_, n * CH:(n + 1) * CH],
                             start=False, stop=(n == 31), skip_group_check=True)
            b = 2 * (n % 2) + hh
            ps = k.take(b)
            t = matmuls(k, ps[rows_, 0:64], [(MT[rows_, n, :], S[rows_, n, :])])
            if k.dve.behind(t):
                nc.vector.wait_ge(*t)
            last[hh] = k.dve.mark(nc.vector.tensor_tensor(S[rows_, n + 1, :], ps[rows_, 0:64], N[rows_, n, :], ALU.add).then_inc(k.dve_done, 1))
            k.bank_read[b].append(last[hh])
    y, cen = e1, e2
    if k.act.behind(k.pe.last()):
        nc.scalar.wait_ge(*k.pe.last())
    if k.act.behind(k.dve.last()):
        nc.scalar.wait_ge(*k.dve.last())
    for hh in range(2):
        rows_ = slice(64 * hh, 64 * hh + 64)
        t = k.act.mark(nc.scalar.copy(y[rows_], k.bank[4 + hh][rows_, :]).then_inc(k.act_done, 1))
        k.bank_read[4 + hh].append(t)
    def head_sum(src):
        b = k.next_bank()
        ps = k.take(b)
        if k.pe.behind(k.dve.last()):
            nc.tensor.wait_ge(*k.dve.last())
        if k.pe.behind(k.act.last()):
            nc.tensor.wait_ge(*k.act.last())
        t = matmuls(k, ps[:, :], [(s.c("halves"), src)])
        if k.dve.behind(t):
            nc.vector.wait_ge(*t)
        if k.act.behind(t):
            nc.scalar.wait_ge(*t)
        return b, ps
    b, ps = head_sum(y)
    k.bank_read[b].append(k.dve.mark(nc.vector.scalar_tensor_tensor(cen, ps[:, :], -1.0 / 64, y, ALU.mult, ALU.add).then_inc(k.dve_done, 1)))
    nc.vector.wait_ge(*k.dve.last())
    k.dve.mark(nc.vector.tensor_tensor(y, cen, cen, ALU.mult).then_inc(k.dve_done, 1))
    nc.vector.wait_ge(*k.dve.last())
    b, ps = head_sum(y)
    t = k.act.mark(nc.scalar.activation(y, ps[:, :], ACT.Sqrt, bias=s.c("eps")[:, 2:3], scale=1.0 / 64).then_inc(k.act_done, 1))
    k.bank_read[b].append(t)
    if k.dve.behind(t):
        nc.vector.wait_ge(*t)
    k.dve.mark(nc.vector.reciprocal(y, y).then_inc(k.dve_done, 1))
    nc.vector.wait_ge(*k.dve.last())
    k.dve.mark(nc.vector.scalar_tensor_tensor(cen, cen, par("c_gn_w"), y, ALU.mult, ALU.mult).then_inc(k.dve_done, 1))
    nc.vector.wait_ge(*k.dve.last())
    k.dve.mark(nc.vector.scalar_tensor_tensor(y, r, par("c_rk"), kmod, ALU.mult, ALU.mult).then_inc(k.dve_done, 1))
    nc.vector.wait_ge(*k.dve.last())
    b, ps = head_sum(y)
    k.bank_read[b].append(k.dve.mark(nc.vector.tensor_tensor(y, ps[:, :], v, ALU.mult).then_inc(k.dve_done, 1)))
    nc.vector.wait_ge(*k.dve.last())
    k.dve.mark(nc.vector.scalar_tensor_tensor(cen, cen, par("c_gn_b"), y, ALU.add, ALU.add).then_inc(k.dve_done, 1))
    nc.vector.wait_ge(*k.dve.last())
    k.dve.mark(nc.vector.tensor_tensor(s.branch[:, 4 + m, :], cen, gate, ALU.mult).then_inc(k.dve_done, 1))
    k.fence()


def turn4(k, s, src, dst, dst2=None):
    nc = k.nc
    b = k.next_bank(low=True)
    ps = k.take(b)
    for tt in range(NTL):
        t = k.pe.mark(nc.tensor.transpose(ps[:, tt * P:(tt + 1) * P], src[:, tt * P:(tt + 1) * P], s.c("ident")).then_inc(k.pe_done, 1))
    view = ps[:, 0:512].rearrange("p (a c) -> p a c", a=NTL)
    if dst2 is None:
        return k.evac(b, dst, view, t)
    k.evac(b, dst2[0], view[:, :, 0:64], t)
    return k.evac(b, dst2[1], view[:, :, 64:128], t, same=True)


def mamba_mixer(k, s):
    nc = k.nc
    A = s.arena
    mark = A.mark()
    z = A.take([2, LAT])
    raw = A.take([4, LAT])
    xbc = A.take([4, LAT])
    dt = A.take([NTL, 4])
    tiny = A.take([8, 16])
    x_tok = A.take([2, NTL, P])
    b_tok = A.take([NTL, P])
    bd = A.take([4, 64])
    diag = A.take([512])
    lane = A.take([512])
    dec = A.take([512])
    ch = A.take([512])
    S = A.take([2, 2, 64])
    y = A.take([2, LAT])
    k.fence()
    into_features(k, s, "d_z", 256, z)
    into_features(k, s, "d_xbc", 512, raw)
    into_tokens(k, s, "d_dt", 4, dt)
    k.fence()
    w = lambda tap, i: s.p("d_conv_w")[:, tap * 4 + i:tap * 4 + i + 1]
    for i in range(4):
        k.dve.mark(nc.vector.tensor_scalar(xbc[:, i, :], raw[:, i, :], w(3, i), s.p("d_conv_b")[:, i:i + 1], ALU.mult, ALU.add).then_inc(k.dve_done, 1))
        nc.vector.wait_ge(*k.dve.last())
        for tap in range(3):
            back = 3 - tap
            k.dve.mark(nc.vector.scalar_tensor_tensor(xbc[:, i, back:LAT], raw[:, i, 0:LAT - back], w(tap, i),
                                                      xbc[:, i, back:LAT], ALU.mult, ALU.add).then_inc(k.dve_done, 1))
            nc.vector.wait_ge(*k.dve.last())
    if k.act.behind(k.dve.last()):
        nc.scalar.wait_ge(*k.dve.last())
    k.act.mark(nc.scalar.activation(xbc[:, :, :], xbc[:, :, :], ACT.Silu).then_inc(k.act_done, 1))
    k.act.mark(nc.scalar.activation(z[:, :, :], z[:, :, :], ACT.Silu).then_inc(k.act_done, 1))
    x, u, w1, ln, den, zero, a, da = (tiny[:, i, :] for i in range(8))
    heads = lambda v: v.rearrange("p (t h) -> p t h", h=4)
    k.dve.mark(nc.vector.tensor_tensor(heads(x), dt[:, :, :], repeat(s.p("d_dt_bias"), NTL), ALU.add).then_inc(k.dve_done, 1))
    if k.act.behind(k.dve.last()):
        nc.scalar.wait_ge(*k.dve.last())
    k.act.mark(nc.scalar.activation(u, x, ACT.Abs).then_inc(k.act_done, 1))
    nc.scalar.wait_ge(*k.act.last())
    k.act.mark(nc.scalar.activation(u, u, ACT.Exp, scale=-1.0).then_inc(k.act_done, 1))
    nc.scalar.wait_ge(*k.act.last())
    if k.dve.behind(k.act.last()):
        nc.vector.wait_ge(*k.act.last())
    if k.dve.behind(k.dve.last()):
        nc.vector.wait_ge(*k.dve.last())
    k.dve.mark(nc.vector.tensor_scalar(w1, u, 1.0, None, ALU.add).then_inc(k.dve_done, 1))
    nc.vector.wait_ge(*k.dve.last())
    if k.act.behind(k.dve.last()):
        nc.scalar.wait_ge(*k.dve.last())
    k.act.mark(nc.scalar.activation(ln, w1, ACT.Ln).then_inc(k.act_done, 1))
    nc.scalar.wait_ge(*k.act.last())
    k.act.mark(nc.scalar.activation(a[:, 0:4], s.p("d_a_log"), ACT.Exp).then_inc(k.act_done, 1))
    if k.dve.behind(k.act.last()):
        nc.vector.wait_ge(*k.act.last())
    k.dve.mark(nc.vector.tensor_scalar(den, w1, -1.0, None, ALU.add).then_inc(k.dve_done, 1))
    nc.vector.wait_ge(*k.dve.last())
    k.dve.mark(nc.vector.tensor_scalar(zero, den, 0.0, None, ALU.is_equal).then_inc(k.dve_done, 1))
    nc.vector.wait_ge(*k.dve.last())
    k.dve.mark(nc.vector.tensor_tensor(den, den, zero, ALU.add).then_inc(k.dve_done, 1))
    nc.vector.wait_ge(*k.dve.last())
    k.dve.mark(nc.vector.tensor_tensor(ln, ln, zero, ALU.add).then_inc(k.dve_done, 1))
    nc.vector.wait_ge(*k.dve.last())
    k.dve.mark(nc.vector.reciprocal(den, den).then_inc(k.dve_done, 1))
    nc.vector.wait_ge(*k.dve.last())
    k.dve.mark(nc.vector.tensor_tensor(ln, ln, den, ALU.mult).then_inc(k.dve_done, 1))
    nc.vector.wait_ge(*k.dve.last())
    k.dve.mark(nc.vector.tensor_tensor(ln, ln, u, ALU.mult).then_inc(k.dve_done, 1))
    nc.vector.wait_ge(*k.dve.last())
    k.dve.mark(nc.vector.scalar_tensor_tensor(x, x, 0.0, ln, ALU.max, ALU.add).then_inc(k.dve_done, 1))
    nc.vector.wait_ge(*k.dve.last())
    k.dve.mark(nc.vector.scalar_tensor_tensor(heads(da), heads(x), -1.0, repeat(a[:, 0:4], NTL), ALU.mult, ALU.mult).then_inc(k.dve_done, 1))
    dt_v = x
    k.fence()
    acs, to_end, whole = u, w1, ln
    b = k.next_bank()
    ps = k.take(b)
    matmuls(k, ps[:, 0:16], [(s.c("tri"), da)])
    matmuls(k, ps[:, 16:32], [(s.c("tri_after"), da)])
    t = matmuls(k, ps[:, 32:48], [(s.c("ones"), da)])
    if k.act.behind(t):
        nc.scalar.wait_ge(*t)
    k.act.mark(nc.scalar.copy(acs, ps[:, 0:16]).then_inc(k.act_done, 1))
    k.act.mark(nc.scalar.activation(to_end, ps[:, 16:32], ACT.Exp).then_inc(k.act_done, 1))
    k.bank_read[b].append(k.act.mark(nc.scalar.activation(whole, ps[:, 32:48], ACT.Exp).then_inc(k.act_done, 1)))
    for i in range(2):
        turn4(k, s, xbc[:, i, :], x_tok[:, i])
    turn4(k, s, xbc[:, 2, :], b_tok)
    k.fence()
    k.dve.mark(nc.vector.memset(S[:, 0, :, :], 0.0).then_inc(k.dve_done, 1))
    for h in range(4):
        xh = x_tok[:, h // 2, :, 64 * (h % 2):64 * (h % 2) + 64]
        k.dve.mark(nc.vector.tensor_tensor(xh, xh, dt_v.rearrange("p (t h a) -> p t h a", h=4, a=1)[:, :, h, :].to_broadcast([P, NTL, 64]), ALU.mult).then_inc(k.dve_done, 1))
    if k.dve.behind(k.dve.last()):
        nc.vector.wait_ge(*k.dve.last())
    for c in range(NTL):
        cols = slice(c * P, (c + 1) * P)
        col = lambda v, h: v[:, c * 4 + h:c * 4 + h + 1]
        acs_c = acs[:, c * 4:c * 4 + 4].rearrange("p (h a) -> p h a", a=1).to_broadcast([P, 4, P])
        v4 = lambda v: v.rearrange("p (h l) -> p h l", h=4)
        k.fence()
        k.dve.mark(nc.vector.tensor_tensor(v4(diag), repeat(s.c("ident"), 4), acs_c, ALU.mult).then_inc(k.dve_done, 1))
        nc.vector.wait_ge(*k.dve.last())
        ps = k.take(0)
        if k.pe.behind(k.dve.last()):
            nc.tensor.wait_ge(*k.dve.last())
        t = matmuls(k, ps[:, :], [(s.c("ones"), diag)])
        if k.act.behind(t):
            nc.scalar.wait_ge(*t)
        t = k.act.mark(nc.scalar.activation(lane, ps[:, :], ACT.Exp).then_inc(k.act_done, 1))
        if k.dve.behind(t):
            nc.vector.wait_ge(*t)
        k.dve.mark(nc.vector.tensor_tensor(v4(dec), v4(ps[:, 0:512]), acs_c, ALU.subtract).then_inc(k.dve_done, 1))
        nc.vector.wait_ge(*k.dve.last())
        k.bank_read[0].append(k.dve.last())
        k.dve.mark(nc.vector.tensor_scalar(dec, dec, 0.0, None, ALU.min).then_inc(k.dve_done, 1))
        nc.vector.wait_ge(*k.dve.last())
        if k.act.behind(k.dve.last()):
            nc.scalar.wait_ge(*k.dve.last())
        k.act.mark(nc.scalar.activation(dec, dec, ACT.Exp).then_inc(k.act_done, 1))
        if k.dve.behind(k.act.last()):
            nc.vector.wait_ge(*k.act.last())
        k.dve.mark(nc.vector.tensor_tensor(v4(dec), v4(dec), repeat(s.c("tri"), 4), ALU.mult).then_inc(k.dve_done, 1))
        nc.vector.wait_ge(*k.dve.last())
        for g in range(2):
            n_ = slice(64 * g, 64 * g + 64)
            psg = k.take(1 + g)
            t = matmuls(k, psg[:, 0:P], [(xbc[n_, 2, cols], xbc[n_, 3, cols])])
            if k.dve.behind(t):
                nc.vector.wait_ge(*t)
            for h in (2 * g, 2 * g + 1):
                t = k.dve.mark(nc.vector.tensor_tensor(dec[:, h * P:(h + 1) * P], dec[:, h * P:(h + 1) * P], psg[:, 0:P], ALU.mult).then_inc(k.dve_done, 1))
                k.dve.mark(nc.vector.tensor_tensor(ch[n_, h * P:(h + 1) * P], lane[n_, h * P:(h + 1) * P], xbc[n_, 3, cols], ALU.mult).then_inc(k.dve_done, 1))
            k.bank_read[1 + g].append(t)
        for h in range(4):
            g = h // 2
            k.dve.mark(nc.vector.tensor_scalar(bd[:, h, :], b_tok[:, c, 64 * g:64 * g + 64], col(to_end, h), None, ALU.mult).then_inc(k.dve_done, 1))
        if k.pe.behind(k.dve.last()):
            nc.tensor.wait_ge(*k.dve.last())
        for h in range(4):
            g = h // 2
            n_ = slice(64 * g, 64 * g + 64)
            o = slice(64 * (h % 2), 64 * (h % 2) + 64)
            po = k.take(3 + g)
            xh = x_tok[:, h // 2, c, 64 * (h % 2):64 * (h % 2) + 64]
            nc.tensor.matmul(po[o, 0:P], xh, dec[:, h * P:(h + 1) * P], start=True, stop=False)
            t = k.pe.mark(nc.tensor.matmul(po[o, 0:P], S[n_, c % 2, h % 2, :], ch[n_, h * P:(h + 1) * P], start=False, stop=True).then_inc(k.pe_done, 1))
            pst = k.take(5 + g)
            t = matmuls(k, pst[n_, 64 * (h % 2):64 * (h % 2) + 64], [(bd[:, h, :], xh)])
            if h % 2:
                if k.dve.behind(t):
                    nc.vector.wait_ge(*t)
                k.bank_read[3 + g].append(k.dve.mark(nc.vector.tensor_copy(y[:, g, cols], po[:, 0:P]).then_inc(k.dve_done, 1)))
                for hh in range(2):
                    k.bank_read[5 + g].append(k.dve.mark(nc.vector.scalar_tensor_tensor(
                        S[n_, 1 - c % 2, hh, :], S[n_, c % 2, hh, :], whole[n_, c * 4 + 2 * g + hh:c * 4 + 2 * g + hh + 1],
                        pst[n_, 64 * hh:64 * hh + 64], ALU.mult, ALU.add).then_inc(k.dve_done, 1)))
    k.fence()
    for i in range(2):
        k.dve.mark(nc.vector.scalar_tensor_tensor(y[:, i, :], xbc[:, i, :], s.p("d_skip")[:, i:i + 1], y[:, i, :], ALU.mult, ALU.add).then_inc(k.dve_done, 1))
        nc.vector.wait_ge(*k.dve.last())
        k.dve.mark(nc.vector.tensor_tensor(y[:, i, :], y[:, i, :], z[:, i, :], ALU.mult).then_inc(k.dve_done, 1))
        nc.vector.wait_ge(*k.dve.last())
        k.dve.mark(nc.vector.tensor_tensor(raw[:, i, :], y[:, i, :], y[:, i, :], ALU.mult).then_inc(k.dve_done, 1))
        nc.vector.wait_ge(*k.dve.last())
        parts = sum_partitions(k, s, s.c("ones"), raw, LAT, [i], [k.dve.last()])
        inverse_root(k, s, raw[:, 2 + i, :], parts, 1.0 / P, s.c("eps")[:, 1:2])
        if k.dve.behind(k.dve.last()):
            nc.vector.wait_ge(*k.dve.last())
        k.dve.mark(nc.vector.scalar_tensor_tensor(s.branch[:, 6 + i, :], y[:, i, :], s.p("d_norm_w")[:, i:i + 1], raw[:, 2 + i, :], ALU.mult, ALU.mult).then_inc(k.dve_done, 1))
    k.fence()
    A.reset(mark)


def layer_norm(k, s, x, gain, shift, out):
    nc = k.nc
    A = s.arena
    mark = A.mark()
    sq = A.take([KT, LAT])
    mean = A.take([LAT])
    k.fence()
    (b, ps, _, _, t), = sum_partitions(k, s, s.c("ones"), x, LAT, range(KT), [])
    if k.act.behind(t):
        nc.scalar.wait_ge(*t)
    t = k.act.mark(nc.scalar.activation(mean, ps, ACT.Copy, scale=1.0 / D).then_inc(k.act_done, 1))
    k.bank_read[b].append(t)
    if k.dve.behind(t):
        nc.vector.wait_ge(*t)
    k.dve.mark(nc.vector.tensor_tensor(x[:, :, :], x[:, :, :], repeat(mean, KT), ALU.subtract).then_inc(k.dve_done, 1))
    nc.vector.wait_ge(*k.dve.last())
    if k.act.behind(k.dve.last()):
        nc.scalar.wait_ge(*k.dve.last())
    t = k.act.mark(nc.scalar.activation(sq[:, :, :], x[:, :, :], ACT.Square).then_inc(k.act_done, 1))
    parts = sum_partitions(k, s, s.c("ones"), sq, LAT, range(KT), [t])
    t = inverse_root(k, s, mean, parts, 1.0 / D, s.c("eps")[:, 1:2])
    if k.dve.behind(t):
        nc.vector.wait_ge(*t)
    for i in range(KT):
        k.dve.mark(nc.vector.scalar_tensor_tensor(x[:, i, :], x[:, i, :], s.p(gain)[:, i:i + 1], mean, ALU.mult, ALU.mult).then_inc(k.dve_done, 1))
        if k.act.behind(k.dve.last()):
            nc.scalar.wait_ge(*k.dve.last())
        k.act.mark(nc.scalar.activation(out[:, i, :], x[:, i, :], ACT.Identity, bias=s.p(shift)[:, i:i + 1]).then_inc(k.act_done, 1))
    k.fence()
    A.reset(mark)


def merge_branches(k, s):
    nc = k.nc
    A = s.arena
    mark = A.mark()
    merged = A.take([KT, LAT])
    pre = A.take([KT, LAT])
    sig = A.take([2, LAT])
    prod = A.take([2, LAT])
    wb = s.d["w_branch_2"]
    k.fence()
    turn_ = 0
    sig_used, prod_used = [None, None], [None, None]
    added = {}
    for n in range(4):
        for c0 in range(0, D, 256):
            first = SEG["gates"] + n * D + c0
            wg, tg, sg = k.load(s.d["w_in_2"][:, first:first + 256].rearrange("(t p) c -> p t c", p=P), KT, 256)
            wbr, tb, sb_ = k.load(wb[n, :, c0:c0 + 256].rearrange("(t p) c -> p t c", p=P), 2, 256)
            for m in range(2):
                mt = c0 // P + m
                e = turn_ % 2
                turn_ += 1
                bg = k.next_bank()
                psg = k.take(bg)
                if k.pe.behind(tg):
                    nc.tensor.wait_ge(*tg)
                t = matmuls(k, psg[:, :], [(wg[:, i, m * P:(m + 1) * P], s.hT[:, i, 0:LAT]) for i in range(KT)])
                bb = k.next_bank()
                psb = k.take(bb)
                if k.pe.behind(tb):
                    nc.tensor.wait_ge(*tb)
                tb2 = matmuls(k, psb[:, :], [(wbr[:, i, m * P:(m + 1) * P], s.branch[:, 2 * n + i, :]) for i in range(2)])
                if k.act.behind(t):
                    nc.scalar.wait_ge(*t)
                if sig_used[e]:
                    if k.act.behind(sig_used[e]):
                        nc.scalar.wait_ge(*sig_used[e])
                t = k.act.mark(nc.scalar.activation(sig[:, e, :], psg[:, :], ACT.Sigmoid).then_inc(k.act_done, 1))
                k.bank_read[bg].append(t)
                if k.dve.behind(t):
                    nc.vector.wait_ge(*t)
                if k.dve.behind(tb2):
                    nc.vector.wait_ge(*tb2)
                if n == 0:
                    t = k.dve.mark(nc.vector.tensor_tensor(merged[:, mt, :], sig[:, e, :], psb[:, :], ALU.mult).then_inc(k.dve_done, 1))
                    sig_used[e] = t
                else:
                    if prod_used[e]:
                        if k.dve.behind(prod_used[e]):
                            nc.vector.wait_ge(*prod_used[e])
                    t = k.dve.mark(nc.vector.tensor_tensor(prod[:, e, :], sig[:, e, :], psb[:, :], ALU.mult).then_inc(k.dve_done, 1))
                    sig_used[e] = t
                    if k.pool.behind(t):
                        nc.gpsimd.wait_ge(*t)
                    if k.pool.behind(added[mt]):
                        nc.gpsimd.wait_ge(*added[mt])
                    prod_used[e] = k.pool.mark(nc.gpsimd.tensor_tensor(merged[:, mt, :], merged[:, mt, :], prod[:, e, :], ALU.add).then_inc(k.pool_done, 1))
                k.bank_read[bb].append(t)
                added[mt] = prod_used[e] if n else t
            k.free(sg)
            k.free(sb_)
    k.fence()
    for c0 in range(0, D, 256):
        tiles = []
        for m in range(2):
            mt = c0 // P + m

            def add(ps, t0, t1, t, mt=mt):
                if k.dve.behind(t):
                    nc.vector.wait_ge(*t)
                return [k.dve.mark(nc.vector.scalar_tensor_tensor(pre[:, mt, :], s.hT[:, mt, 0:LAT], ALPHA, ps, ALU.mult, ALU.add).then_inc(k.dve_done, 1))]
            tiles.append((c0 + m * P, P, (0, LAT), add))
        project_features(k, s.d["w_out_2"], (c0, c0 + 256), merged, LAT, tiles, [])
    layer_norm(k, s, pre, "ln1_g", "ln1_b", s.hT[:, :, 0:LAT])
    A.reset(mark)


def second_block(k, s, out):
    nc = k.nc
    s.branch = s.xT[:, :, 0:LAT]
    s.arena.reset(0)
    s.after_job = None
    dilated_attention(k, s)
    indexed_attention(k, s)
    rwkv_mixer(k, s)
    mamba_mixer(k, s)
    merge_branches(k, s)
    mixture_of_experts(k, s, out)


class LoopEngine:

    def __init__(self, sem, per):
        self.sem, self.per, self.n = sem, per, 0

    def mark(self, ins):
        self.n += 1
        return (self, self.n)


def in_round(i, ticket):
    e, n = ticket
    return e.sem, i * e.per + (e.per + n)


def first_maximum(k, one, vals, m, iota, scratch, idx):
    nc = k.nc
    n = vals.shape[-1]
    up = lambda v: v.rearrange("p (t a) -> p t a", a=1).to_broadcast([P, NTL, n])
    k.dve.mark(nc.vector.tensor_reduce(m, vals, AX.X, ALU.max).then_inc(k.dve_done, 1))
    nc.vector.wait_ge(*k.dve.last())
    k.dve.mark(nc.vector.tensor_tensor(scratch, vals, up(m), ALU.is_equal).then_inc(k.dve_done, 1))
    nc.vector.wait_ge(*k.dve.last())
    k.dve.mark(nc.vector.scalar_tensor_tensor(scratch, scratch, -99.0, repeat(iota, NTL), ALU.mult, ALU.add).then_inc(k.dve_done, 1))
    nc.vector.wait_ge(*k.dve.last())
    k.dve.mark(nc.vector.tensor_reduce(idx, scratch, AX.X, ALU.min).then_inc(k.dve_done, 1))
    nc.vector.wait_ge(*k.dve.last())
    k.dve.mark(nc.vector.tensor_tensor(one, scratch, up(idx), ALU.is_equal).then_inc(k.dve_done, 1))
    nc.vector.wait_ge(*k.dve.last())


def mixture_of_experts(k, s, out):
    nc = k.nc
    A = s.arena
    A.reset(0)
    w = A.take([2, 3, SLOT * 2])
    k.fence()
    x = s.hT
    x_tok = k.ring[:, 0:2, :].rearrange("p s n -> p (s n)").rearrange("p (t n) -> p t n", t=NTL)
    spare = k.ring[:, 2:4, :].rearrange("p s n -> p (s n)")
    rel, gates = A.take([2, 4]), A.take([2, 4])
    blk_i = k.ctx.enter_context(nc.sbuf_tensor("block_expert", [1, 48], I32))
    for half in range(2):
        for tt in range(NTL):
            b = k.next_bank()
            ps = k.take(b)
            for m in range(4):
                t = k.pe.mark(nc.tensor.transpose(ps[:, m * P:(m + 1) * P], x[:, 4 * half + m, tt * P:(tt + 1) * P], s.c("ident")).then_inc(k.pe_done, 1))
            k.evac(b, x_tok[:, tt, half * 512:half * 512 + 512], ps[:, :], t)
    R = w[:, 0, 0, :]
    at = [0]

    def small(*shape):
        n = int(np.prod(shape))
        v = R[:, at[0]:at[0] + n]
        at[0] += n
        return v.rearrange("p (a b) -> p a b", a=shape[0]) if len(shape) == 2 else v
    L, pen, eg, le, sc = small(NTL, 36), small(NTL, 4), small(NTL, 4), small(NTL, 32), small(NTL, 32)
    o1, o2, o12, base, og = small(NTL, 32), small(NTL, 32), small(NTL, 32), small(NTL, 32), small(NTL, 4)
    mg, idx, pg, m1, m2, ex, den = (small(NTL) for _ in range(7))
    nb, incl, start, cnt = (small(32) for _ in range(4))
    blk, pairs = small(40), small(4)
    b = k.next_bank()
    ps = k.take(b)
    rw = s.p("router_w").rearrange("p (t n) -> p t n", t=KT)
    for tt in range(NTL):
        t = matmuls(k, ps[:, tt * 36:(tt + 1) * 36], [(x[:, i, tt * P:(tt + 1) * P], rw[:, i, :]) for i in range(KT)])
    if k.dve.behind(t):
        nc.vector.wait_ge(*t)
    k.bank_read[b].append(k.dve.mark(nc.vector.tensor_tensor(L, ps[:, 0:144].rearrange("p (t n) -> p t n", t=NTL), repeat(s.p("router_b"), NTL), ALU.add).then_inc(k.dve_done, 1)))
    nc.vector.wait_ge(*k.dve.last())
    up = lambda v, n: v.rearrange("p (t a) -> p t a", a=1).to_broadcast([P, NTL, n])
    first_maximum(k, og, L[:, :, 0:4], mg, s.c("expert")[:, 0:4], pen, idx)
    k.dve.mark(nc.vector.tensor_tensor(eg, L[:, :, 0:4], up(mg, 4), ALU.subtract).then_inc(k.dve_done, 1))
    nc.vector.wait_ge(*k.dve.last())
    if k.act.behind(k.dve.last()):
        nc.scalar.wait_ge(*k.dve.last())
    k.act.mark(nc.scalar.activation(eg, eg, ACT.Exp).then_inc(k.act_done, 1))
    if k.dve.behind(k.act.last()):
        nc.vector.wait_ge(*k.act.last())
    k.dve.mark(nc.vector.tensor_reduce(pg, eg, AX.X, ALU.add).then_inc(k.dve_done, 1))
    nc.vector.wait_ge(*k.dve.last())
    k.dve.mark(nc.vector.reciprocal(pg, pg).then_inc(k.dve_done, 1))
    nc.vector.wait_ge(*k.dve.last())
    k.dve.mark(nc.vector.tensor_scalar(pen, og, 1.0, -NEG, ALU.subtract, ALU.mult).then_inc(k.dve_done, 1))
    nc.vector.wait_ge(*k.dve.last())
    for g in range(4):
        k.dve.mark(nc.vector.tensor_tensor(le[:, :, 8 * g:8 * g + 8], L[:, :, 4 + 8 * g:12 + 8 * g], pen[:, :, g:g + 1].to_broadcast([P, NTL, 8]), ALU.add).then_inc(k.dve_done, 1))
        nc.vector.wait_ge(*k.dve.last())
    first_maximum(k, o1, le, m1, s.c("expert"), sc, idx)
    k.dve.mark(nc.vector.scalar_tensor_tensor(le, o1, 2 * NEG, le, ALU.mult, ALU.add).then_inc(k.dve_done, 1))
    nc.vector.wait_ge(*k.dve.last())
    first_maximum(k, o2, le, m2, s.c("expert"), sc, idx)
    k.dve.mark(nc.vector.tensor_tensor(ex, m2, m1, ALU.subtract).then_inc(k.dve_done, 1))
    nc.vector.wait_ge(*k.dve.last())
    if k.act.behind(k.dve.last()):
        nc.scalar.wait_ge(*k.dve.last())
    k.act.mark(nc.scalar.activation(ex, ex, ACT.Exp).then_inc(k.act_done, 1))
    if k.dve.behind(k.act.last()):
        nc.vector.wait_ge(*k.act.last())
    k.dve.mark(nc.vector.tensor_scalar(den, ex, 1.0, None, ALU.add).then_inc(k.dve_done, 1))
    nc.vector.wait_ge(*k.dve.last())
    k.dve.mark(nc.vector.reciprocal(den, den).then_inc(k.dve_done, 1))
    nc.vector.wait_ge(*k.dve.last())
    k.dve.mark(nc.vector.tensor_tensor(gates[:, 0, :], pg, den, ALU.mult).then_inc(k.dve_done, 1))
    nc.vector.wait_ge(*k.dve.last())
    k.dve.mark(nc.vector.tensor_tensor(gates[:, 1, :], gates[:, 0, :], ex, ALU.mult).then_inc(k.dve_done, 1))
    nc.vector.wait_ge(*k.dve.last())
    k.dve.mark(nc.vector.tensor_tensor(o12, o1, o2, ALU.add).then_inc(k.dve_done, 1))
    nc.vector.wait_ge(*k.dve.last())
    b = k.next_bank()
    ps = k.take(b)
    if k.pe.behind(k.dve.last()):
        nc.tensor.wait_ge(*k.dve.last())
    for tt in range(NTL):
        matmuls(k, ps[:, tt * 32:(tt + 1) * 32], [(s.c("tri_before"), o12[:, tt, :])] + [(s.c("ones"), o12[:, u, :]) for u in range(tt)])
    t = matmuls(k, ps[:, 128:160], [(s.c("ones"), o12[:, tt, :]) for tt in range(NTL)])
    if k.dve.behind(t):
        nc.vector.wait_ge(*t)
    k.dve.mark(nc.vector.tensor_copy(cnt, ps[:, 128:160]).then_inc(k.dve_done, 1))
    nc.vector.wait_ge(*k.dve.last())
    k.dve.mark(nc.vector.tensor_scalar(nb, cnt, 0.0, None, ALU.is_gt).then_inc(k.dve_done, 1))
    nc.vector.wait_ge(*k.dve.last())
    for m in range(1, NTL):
        k.dve.mark(nc.vector.scalar_tensor_tensor(nb, cnt, float(m * P), nb, ALU.is_gt, ALU.add).then_inc(k.dve_done, 1))
        nc.vector.wait_ge(*k.dve.last())
    k.dve.mark(nc.vector.tensor_tensor_scan(incl, s.c("ones")[:, 0:32], nb, 0.0, ALU.mult, ALU.add).then_inc(k.dve_done, 1))
    nc.vector.wait_ge(*k.dve.last())
    k.dve.mark(nc.vector.tensor_tensor(start, incl, nb, ALU.subtract).then_inc(k.dve_done, 1))
    nc.vector.wait_ge(*k.dve.last())
    k.dve.mark(nc.vector.tensor_scalar(start, start, float(P), None, ALU.mult).then_inc(k.dve_done, 1))
    nc.vector.wait_ge(*k.dve.last())
    k.bank_read[b].append(k.dve.mark(nc.vector.tensor_tensor(base, ps[:, 0:128].rearrange("p (t n) -> p t n", t=NTL), repeat(start, NTL), ALU.add).then_inc(k.dve_done, 1)))
    nc.vector.wait_ge(*k.dve.last())
    for j, o in enumerate((o1, o2)):
        k.dve.mark(nc.vector.tensor_tensor(sc, o, base, ALU.mult).then_inc(k.dve_done, 1))
        nc.vector.wait_ge(*k.dve.last())
        k.dve.mark(nc.vector.tensor_reduce(rel[:, j, :], sc, AX.X, ALU.add).then_inc(k.dve_done, 1))
        nc.vector.wait_ge(*k.dve.last())
    cmp_ = w[:, 0, 1, 0:1280].rearrange("p (n e) -> p n e", e=32)
    nth = s.c("iota")[:, 0:40].rearrange("p (n a) -> p n a", a=1).to_broadcast([P, 40, 32])
    k.dve.mark(nc.vector.tensor_tensor(cmp_, repeat(incl, 40), nth, ALU.is_le).then_inc(k.dve_done, 1))
    nc.vector.wait_ge(*k.dve.last())
    k.dve.mark(nc.vector.tensor_reduce(blk, cmp_, AX.X, ALU.add).then_inc(k.dve_done, 1))
    nc.vector.wait_ge(*k.dve.last())
    k.dve.mark(nc.vector.tensor_scalar(blk, blk, 31.0, None, ALU.min).then_inc(k.dve_done, 1))
    nc.vector.wait_ge(*k.dve.last())
    k.dve.mark(nc.vector.tensor_copy(blk_i[0:1, 0:40], blk[0:1, :]).then_inc(k.dve_done, 1))
    nc.vector.wait_ge(*k.dve.last())
    k.dve.mark(nc.vector.tensor_scalar(cmp_[:, 0, 0:20], s.c("iota")[:, 0:40:2], incl[:, 31:32], None, ALU.is_lt).then_inc(k.dve_done, 1))
    nc.vector.wait_ge(*k.dve.last())
    k.dve.mark(nc.vector.tensor_reduce(pairs[:, 0:1], cmp_[:, 0, 0:20], AX.X, ALU.add).then_inc(k.dve_done, 1))
    nc.vector.wait_ge(*k.dve.last())
    k.dve.mark(nc.vector.tensor_copy(blk_i[0:1, 44:45], pairs[0:1, 0:1]).then_inc(k.dve_done, 1))
    nc.vector.wait_ge(*k.dve.last())

    acc = s.xT[:, :, 0:LAT]
    k.dve.mark(nc.vector.memset(acc, 0.0).then_inc(k.dve_done, 1))
    nc.vector.wait_ge(*k.dve.last())
    moved = [s.xT[:, :, LAT + P * u:LAT + P * u + P] for u in range(2)]
    made = [s.hT[:, :, LAT + P * u:LAT + P * u + P] for u in range(2)]
    pieces = [spare[:, 512 * n:512 * n + 512] for n in range(8)]
    back, act_, hid = pieces[0:2], pieces[2:4], pieces[4:6]
    eq1, sel = pieces[6], [pieces[7], A.take([512])]
    eq2 = A.take([512])
    selg = [A.take([512]) for _ in range(2)]

    sem = lambda n: k.ctx.enter_context(nc.semaphore(n))
    PE_N, ACT_N, DVE_N = 2 * (3 + 2 + 2 + KT), 2 * (2 + 1 + 2), 2 * (7 + 1 + 1 + KT)
    pe, act, dve = (LoopEngine(sem(n), c) for n, c in
                    (("pe_loop", PE_N), ("act_loop", ACT_N), ("dve_loop", DVE_N)))
    up_loaded = [sem(f"gate_up{u}_loaded") for u in range(2)]
    down_loaded = [sem(f"down{u}_loaded") for u in range(2)]
    for cell, e in enumerate((pe, act, dve)):
        nc.vector.memset(s.small[0:1, 250 + cell:251 + cell], 0.0).then_inc(e.sem, e.per)
    k.fence()
    if k.sp.behind(k.pe.last()):
        nc.sync.wait_ge(*k.pe.last())
    if k.sp.behind(k.act.last()):
        nc.sync.wait_ge(*k.act.last())
    if k.sp.behind(k.dve.last()):
        nc.sync.wait_ge(*k.dve.last())
    ET = mybir.EngineType
    n_pairs = nc.values_load(blk_i[0:1, 44:45], engines=(ET.PE, ET.Activation, ET.DVE, ET.SP), min_val=1, max_val=20)
    gate_d, up_d, down_d = s.d["e_gate_2"], s.d["e_up_2"], s.d["e_down_2"]
    part = lambda u, n, rows_, cols: w[:, u, n, :].rearrange("p (t c) -> p t c", t=rows_)

    with nc.Fori(0, n_pairs, 1, engines=(ET.PE, ET.Activation, ET.DVE, ET.SP)) as i:
        nc.tensor.wait_ge(act.sem, i * act.per + act.per)
        nc.tensor.wait_ge(dve.sem, i * dve.per + dve.per)
        nc.scalar.wait_ge(pe.sem, i * pe.per + pe.per)
        nc.scalar.wait_ge(dve.sem, i * dve.per + dve.per)
        nc.scalar.wait_ge(act.sem, i * act.per + act.per)
        nc.vector.wait_ge(pe.sem, i * pe.per + pe.per)
        nc.vector.wait_ge(act.sem, i * act.per + act.per)
        nc.vector.wait_ge(dve.sem, i * dve.per + dve.per)
        three = lambda v: v.rearrange("p (t c) -> p t c", t=NTL)
        chosen = []
        slot_no = repeat(s.c("iota"), NTL)
        for u in range(2):
            r1, r2 = up(rel[:, 0, :], P), up(rel[:, 1, :], P)
            dve.mark(nc.vector.tensor_tensor(three(eq1), slot_no, r1, ALU.is_equal).then_inc(dve.sem, 1))
            t = dve.mark(nc.vector.tensor_tensor(three(eq2), slot_no, r2, ALU.is_equal).then_inc(dve.sem, 1))
            nc.vector.wait_ge(*in_round(i, t))
            t = dve.mark(nc.vector.tensor_tensor(sel[u], eq1, eq2, ALU.add).then_inc(dve.sem, 1))
            dve.mark(nc.vector.tensor_scalar(rel[:, :, :], rel[:, :, :], -float(P), None, ALU.add).then_inc(dve.sem, 1))
            nc.vector.wait_ge(*in_round(i, t))
            dve.mark(nc.vector.tensor_tensor(three(eq1), three(eq1), up(gates[:, 0, :], P), ALU.mult).then_inc(dve.sem, 1))
            t2 = dve.mark(nc.vector.tensor_tensor(three(eq2), three(eq2), up(gates[:, 1, :], P), ALU.mult).then_inc(dve.sem, 1))
            nc.vector.wait_ge(*in_round(i, t2))
            t2 = dve.mark(nc.vector.tensor_tensor(selg[u], eq1, eq2, ALU.add).then_inc(dve.sem, 1))
            if u == 0:
                nc.vector.wait_ge(*in_round(i, t2))
            chosen.append((t, t2))
        gather_banks, back_bank = ((0, 1), (5, 6)), (2, 7)
        ready, up_read, down_read = {}, {}, {}
        for u in range(2):
            nc.tensor.wait_ge(*in_round(i, chosen[u][0]))
            for half in range(2):
                ps = k.bank[gather_banks[u][half]]
                for m in range(4):
                    for tt in range(NTL):
                        ins = nc.tensor.matmul(ps[:, m * P:(m + 1) * P], x_tok[:, tt, (4 * half + m) * P:(4 * half + m + 1) * P],
                                               sel[u][:, tt * P:(tt + 1) * P], start=(tt == 0), stop=(tt == NTL - 1))
                t = pe.mark(ins.then_inc(pe.sem, 1))
                nc.scalar.wait_ge(*in_round(i, t))
                ready["moved", u] = act.mark(nc.scalar.copy(moved[u][:, 4 * half:4 * half + 4, :], ps[:, 0:512].rearrange("p (m c) -> p m c", m=4)).then_inc(act.sem, 1))
            nc.tensor.wait_ge(*in_round(i, chosen[u][1]))
            for tt in range(NTL):
                ins = nc.tensor.transpose(k.bank[back_bank[u]][:, tt * P:(tt + 1) * P], selg[u][:, tt * P:(tt + 1) * P], s.c("ident"))
            t = pe.mark(ins.then_inc(pe.sem, 1))
            nc.vector.wait_ge(*in_round(i, t))
            ready["back", u] = dve.mark(nc.vector.tensor_copy(back[u], k.bank[back_bank[u]][:, :]).then_inc(dve.sem, 1))
        up_banks = ((3, 4), (0, 1))
        for u in range(2):
            nc.tensor.wait_ge(up_loaded[u], i * 32 + 32)
            nc.tensor.wait_ge(*in_round(i, ready["moved", u]))
            nc.tensor.wait_ge(*in_round(i, ready["moved", 0]))
            for n in range(2):
                ps = k.bank[up_banks[u][n]]
                for f in range(4):
                    for kt in range(KT):
                        ins = nc.tensor.matmul(ps[:, f * P:(f + 1) * P], part(u, n, KT, 512)[:, kt, f * P:(f + 1) * P],
                                               moved[u][:, kt, :], start=(kt == 0), stop=(kt == KT - 1))
                t = pe.mark(ins.then_inc(pe.sem, 1))
                if n == 0:
                    nc.scalar.wait_ge(*in_round(i, t))
                    ta = act.mark(nc.scalar.activation(act_[u], ps[:, :], ACT.Silu).then_inc(act.sem, 1))
                else:
                    nc.vector.wait_ge(*in_round(i, t))
                    nc.vector.wait_ge(*in_round(i, ta))
                    ready["hid", u] = dve.mark(nc.vector.tensor_tensor(hid[u], act_[u], ps[:, :], ALU.mult).then_inc(dve.sem, 1))
            up_read[u] = t
        down_banks = ((5, 6), (2, 7))
        for u in range(2):
            nc.tensor.wait_ge(down_loaded[u], i * 16 + 16)
            nc.tensor.wait_ge(*in_round(i, ready["hid", u]))
            nc.tensor.wait_ge(*in_round(i, ready["back", u]))
            nc.tensor.wait_ge(*in_round(i, ready["moved", 1]))
            for half in range(2):
                ps = k.bank[down_banks[u][half]]
                for f in range(4):
                    ins = nc.tensor.matmul(ps[:, :], hid[u][:, f * P:(f + 1) * P], part(u, 2, 4, D)[:, f, half * 512:half * 512 + 512],
                                           start=(f == 0), stop=(f == 3))
                t = pe.mark(ins.then_inc(pe.sem, 1))
                nc.scalar.wait_ge(*in_round(i, t))
                down_read[u] = t
                ready["made", u] = act.mark(nc.scalar.copy(made[u][:, 4 * half:4 * half + 4, :], ps[:, 0:512].rearrange("p (m c) -> p m c", m=4)).then_inc(act.sem, 1))
        cyc = (3, 4, 0, 1)
        read = {}
        for u in range(2):
            nc.tensor.wait_ge(*in_round(i, ready["made", u]))
            nc.tensor.wait_ge(*in_round(i, ready["hid", 1]))
            for m in range(KT):
                b = cyc[m % 4]
                if b in read:
                    nc.tensor.wait_ge(*in_round(i, read[b]))
                t = pe.mark(nc.tensor.matmul(k.bank[b][:, :], made[u][:, m, :], back[u], start=True, stop=True).then_inc(pe.sem, 1))
                nc.vector.wait_ge(*in_round(i, t))
                if u:
                    nc.vector.wait_ge(*in_round(i, read["acc", m]))
                read[b] = read["acc", m] = dve.mark(nc.vector.tensor_tensor(acc[:, m, :], acc[:, m, :], k.bank[b][:, :], ALU.add).then_inc(dve.sem, 1))
        for u in range(2):
            e = nc.sync.value_load(blk_i[0:1, bass.ds(i * 2 + u, 1)], min_val=0, max_val=N_EXP - 1)
            nc.sync.wait_ge(pe.sem, i * PE_N + up_read[u][1])
            for n, src in ((0, gate_d), (1, up_d)):
                nc.sync.dma_start(part(u, n, KT, D_EXP), src[bass.ds(e, 1), :, :].rearrange("a (t p) c -> p (a t) c", p=P)).then_inc(up_loaded[u], 16)
            nc.sync.wait_ge(pe.sem, i * PE_N + down_read[u][1])
            nc.sync.dma_start(part(u, 2, 4, D), down_d[bass.ds(e, 1), :, :].rearrange("a (t p) c -> p (a t) c", p=P)).then_inc(down_loaded[u], 16)
        assert (pe.n, act.n, dve.n) == (PE_N, ACT_N, DVE_N), (pe.n, act.n, dve.n)
    nc.all_engine_barrier()
    pre = w[:, 0, 0, :].rearrange("p (t c) -> p t c", t=KT)
    for i in range(KT):
        k.dve.mark(nc.vector.scalar_tensor_tensor(pre[:, i, :], x[:, i, 0:LAT], ALPHA, acc[:, i, :], ALU.mult, ALU.add).then_inc(k.dve_done, 1))
        nc.vector.wait_ge(*k.dve.last())
    A.reset(SLOT * 2)
    layer_norm(k, s, pre, "ln2_g", "ln2_b", acc)
    if k.sp.behind(k.act.last()):
        nc.sync.wait_ge(*k.act.last())
    t = k.stored.mark(nc.sync.dma_start(out.rearrange("(t p) n -> p t n", p=P), acc).then_inc(k.stored.sem, 16))
    if k.sp.behind(t):
        nc.sync.wait_ge(*t)


class Arena:

    def __init__(self, k, words):
        self.t, self.at, self.words = k.sb("arena", [P, words]), 0, words

    def mark(self):
        return self.at

    def reset(self, mark):
        self.at = mark

    def take(self, shape):
        n = int(np.prod(shape))
        assert self.at + n <= self.words, (self.at + n, self.words)
        v = self.t[:, self.at:self.at + n]
        self.at += n
        if len(shape) == 2:
            v = v.rearrange("p (a b) -> p a b", a=shape[0])
        if len(shape) == 3:
            v = v.rearrange("p (a b c) -> p a b c", a=shape[0], b=shape[1])
        return v


def build(nc, d, p_where, c_where, out):
    with ExitStack() as ctx:
        k = Core(nc, ctx)
        s = State()
        s.d = d
        s.params = k.sb("parameters", [P, d["params"].shape[1]])
        s.consts = k.sb("constants", [P, d["consts"].shape[1]])
        s.p = lambda n: s.params[0:p_where[n][1], p_where[n][0]:p_where[n][0] + p_where[n][2]]
        s.c = lambda n: s.consts[0:c_where[n][1], c_where[n][0]:c_where[n][0] + c_where[n][2]]
        s.xT = k.sb("xT", [P, KT, TOK])
        s.hT = k.sb("hT", [P, KT, TOK])
        s.rstd = k.sb("rstd", [P, TOK])
        s.mod = k.sb("mod", [P, 48, 2])
        s.gains = k.sb("gains", [P, 2, KT, 2])
        s.cond = k.sb("cond", [P, KT, 2])
        s.small = k.sb("small", [P, 256])
        s.arena = Arena(k, (nc.sbuf_bytes_remaining - 2048) // 4)
        s.mix = s.arena.take([KT, TOK])
        s.at_used = [None, None]
        s.after_job = None
        s.bias_loaded = [ctx.enter_context(nc.semaphore(f"bias{i}_loaded")) for i in range(2)]
        s.bias_count = [0, 0]
        s.ctx = ctx
        k.params.mark(nc.scalar.dma_start(s.params[:, :], d["params"]).then_inc(k.params.sem, 16))
        k.params.mark(nc.scalar.dma_start(s.consts[:, :], d["consts"]).then_inc(k.params.sem, 16))
        k.params.mark(nc.scalar.dma_start(s.xT[:, :, 0:LAT], d["xT"].rearrange("(t p) n -> p t n", p=P)).then_inc(k.params.sem, 16))
        t = k.params.mark(nc.scalar.dma_start(s.xT[:, :, LAT:TOK], d["ctxT"].rearrange("(t p) n -> p t n", p=P)).then_inc(k.params.sem, 16))
        if k.pe.behind(t):
            nc.tensor.wait_ge(*t)
        if k.act.behind(t):
            nc.scalar.wait_ge(*t)
        if k.dve.behind(t):
            nc.vector.wait_ge(*t)
        if k.pool.behind(t):
            nc.gpsimd.wait_ge(*t)
        s.cond_ready = k.act.mark(nc.scalar.activation(s.cond[:, :, :], s.p("cond").rearrange("p (a b) -> p a b", b=2), ACT.Silu).then_inc(k.act_done, 1))
        first_block(k, s)
        second_block(k, s, out)


def na_bias(rpb):
    col = np.arange(64)
    start = np.clip(col - 8, 0, 48)
    inside = (col[None, :] >= start[:, None]) & (col[None, :] < start[:, None] + 16)
    offset = np.clip(col[None, :] - col[:, None] + 15, 0, 30)
    table = rpb[:, :, :, offset].transpose(0, 1, 3, 2, 4)
    return np.where(inside[:, None, :], table, np.float32(NEG))


def kernel(**inputs):
    import concourse.bacc as _bacc
    from concourse.bass_utils import run_bass_kernel_spmd as _run

    i = {n: np.asarray(a) for n, a in inputs.items()}
    params, p_where = pack(param_columns(i))
    consts, c_where = pack(const_columns())
    arrays = {"params": params, "consts": consts,
              "xT": i["x"][0].T, "ctxT": i["ctx"][0].T, "rpb": na_bias(i["na_rpb"]), "dilated_masks": dilated_masks()}
    for n in ("w_ada", "w_in", "w_out", "ffn_w_up", "ffn_w_down"):
        arrays[n] = i[n]
    for n in ("w_in_2", "w_branch_2", "w_out_2", "e_gate_2", "e_up_2", "e_down_2"):
        arrays[n] = i[n][0]
    arrays = {n: np.ascontiguousarray(a, np.float32) for n, a in arrays.items()}
    nc = _bacc.Bacc("TRN2", target_bir_lowering=False, num_devices=1)
    d = {n: nc.dram_tensor("in_" + n, a.shape, F32, kind="ExternalInput").ap() for n, a in arrays.items()}
    out = nc.dram_tensor("out", (D, LAT), F32, kind="ExternalOutput").ap()
    build(nc, d, p_where, c_where, out)
    r = _run(nc, [{"in_" + n: a for n, a in arrays.items()}], core_ids=[0])
    return np.ascontiguousarray(r.results[0]["out"].T)[None]
```
